# Optimizing a Trainium2 kernel written in Bass

```python
import jax, jax.numpy as jnp
from jax import lax
import numpy as np

D_MODEL = 1024
BATCH = 1
SEQ = 512
DEPTH = 1

CHUNK = 64
MIX_WIDTH = D_MODEL
GM_WIDTH = MIX_WIDTH // 2
GM_BLOCK = 128
GM_GROUPS = 4
GM_CH = GM_WIDTH // GM_GROUPS
MLA_HEADS = 8
QK_NOPE = 64
QK_ROPE = 32
QK_DIM = QK_NOPE + QK_ROPE
V_DIM = 64
MLA_WIDTH = MLA_HEADS * V_DIM
Q_LORA = 384
KV_LORA = 256
ROPE_THETA = 10000.0
Q_BLOCK = 128
IN_COLS = 2 * GM_WIDTH + Q_LORA + KV_LORA + QK_ROPE
N_EXPERTS = 64
TOP_K = 8
N_GROUPS = 8
TOPK_GROUPS = 4
EXPERT_FF = 256
SHARED_FF = 256
ROUTED_SCALE = 2.5
EXPERT_BLOCK = 8
EPS = 1e-6

kernel_name = "hybrid_gmlp_mla_moe_adaln_trunk"

def rms_norm(x, g):
    xf = x.astype(jnp.float32)
    y = xf * lax.rsqrt(jnp.mean(xf * xf, axis=-1, keepdims=True) + EPS)
    return (y * g.astype(jnp.float32)).astype(x.dtype)

def layer_norm(x, g, b):
    xf = x.astype(jnp.float32)
    mu = jnp.mean(xf, axis=-1, keepdims=True)
    xc = xf - mu
    y = xc * lax.rsqrt(jnp.mean(xc * xc, axis=-1, keepdims=True) + EPS)
    return (y * g.astype(jnp.float32) + b.astype(jnp.float32)).astype(x.dtype)

def rope_tables(positions):
    inv_freq = 1.0 / (ROPE_THETA ** (jnp.arange(0, QK_ROPE, 2, dtype=jnp.float32) / QK_ROPE))
    ang = positions.astype(jnp.float32)[..., None] * inv_freq
    return jnp.cos(ang)[:, :, None, :], jnp.sin(ang)[:, :, None, :]

def apply_rope(x, cos, sin):
    xf = x.astype(jnp.float32)
    x1, x2 = jnp.split(xf, 2, axis=-1)
    return jnp.concatenate([x1 * cos - x2 * sin, x1 * sin + x2 * cos], axis=-1).astype(x.dtype)

def gmlp_mixer(uv, ln_g, ln_b, w_s, b_s):
    B, S, _ = uv.shape
    uv = jax.nn.gelu(uv, approximate=False)
    u, v = jnp.split(uv, 2, axis=-1)
    v = v.reshape(B, S // GM_BLOCK, GM_BLOCK, GM_GROUPS, GM_CH)
    v = layer_norm(v, ln_g, ln_b)
    mask = jnp.tril(jnp.ones((GM_BLOCK, GM_BLOCK), dtype=w_s.dtype))
    ws = w_s * mask
    gate = jnp.einsum('gts,bnsgc->bntgc', ws, v) + b_s.T[:, :, None]
    return u * gate.reshape(B, S, GM_WIDTH)

def chunk_causal_attention(q, k, v):
    B, S, H, Dq = q.shape
    nb = S // Q_BLOCK
    scale = QK_DIM ** -0.5
    k_chunk = jnp.arange(S) // CHUNK
    qb = jnp.moveaxis(q.reshape(B, nb, Q_BLOCK, H, Dq), 1, 0)

    def block(args):
        q_blk, i = args
        q_chunk = (i * Q_BLOCK + jnp.arange(Q_BLOCK)) // CHUNK
        s = jnp.einsum('bqhd,bkhd->bhqk', q_blk, k).astype(jnp.float32) * scale
        allowed = k_chunk[None, :] <= q_chunk[:, None]
        s = jnp.where(allowed, s, -jnp.inf)
        p = jax.nn.softmax(s, axis=-1).astype(v.dtype)
        return jnp.einsum('bhqk,bkhd->bqhd', p, v)

    out = lax.map(block, (qb, jnp.arange(nb)))
    return jnp.moveaxis(out, 0, 1).reshape(B, S, H, v.shape[-1])

def mla_mixer(q_lat, kv_lat, k_pe, cos, sin, q_a_g, w_q_up, kv_a_g, w_kv_up, q_norm_g, k_norm_g):
    B, S, _ = q_lat.shape
    q = (rms_norm(q_lat, q_a_g) @ w_q_up).reshape(B, S, MLA_HEADS, QK_DIM)
    kv = (rms_norm(kv_lat, kv_a_g) @ w_kv_up).reshape(B, S, MLA_HEADS, QK_NOPE + V_DIM)
    k_nope, v = kv[..., :QK_NOPE], kv[..., QK_NOPE:]
    k_pe_h = jnp.broadcast_to(k_pe[:, :, None, :], (B, S, MLA_HEADS, QK_ROPE))
    k = jnp.concatenate([k_nope, k_pe_h], axis=-1)
    q = rms_norm(q, q_norm_g)
    k = rms_norm(k, k_norm_g)
    q = jnp.concatenate([q[..., :QK_NOPE], apply_rope(q[..., QK_NOPE:], cos, sin)], axis=-1)
    k = jnp.concatenate([k[..., :QK_NOPE], apply_rope(k[..., QK_NOPE:], cos, sin)], axis=-1)
    out = chunk_causal_attention(q, k, v)
    return out.reshape(B, S, MLA_WIDTH)

def moe_ffn(h, w_router, router_bias, w_gate, w_up, w_down, ws_gate, ws_up, ws_down):
    B, S, D = h.shape
    t = h.reshape(-1, D)
    n_tok = t.shape[0]
    scores = jax.nn.sigmoid((t @ w_router).astype(jnp.float32))
    biased = scores + router_bias.astype(jnp.float32)
    grp = biased.reshape(n_tok, N_GROUPS, N_EXPERTS // N_GROUPS)
    grp_score = jnp.sum(lax.top_k(grp, 2)[0], axis=-1)
    _, gidx = lax.top_k(grp_score, TOPK_GROUPS)
    gmask = jnp.sum(jax.nn.one_hot(gidx, N_GROUPS, dtype=jnp.float32), axis=-2)
    emask = jnp.repeat(gmask, N_EXPERTS // N_GROUPS, axis=-1) > 0
    _, eidx = lax.top_k(jnp.where(emask, biased, -jnp.inf), TOP_K)
    w = jnp.take_along_axis(scores, eidx, axis=-1)
    w = w / jnp.sum(w, axis=-1, keepdims=True) * ROUTED_SCALE
    combine = jnp.sum(jax.nn.one_hot(eidx, N_EXPERTS, dtype=jnp.float32) * w[..., None], axis=1)
    combine = combine.astype(t.dtype)
    routed = jnp.zeros_like(t)
    for e0 in range(0, N_EXPERTS, EXPERT_BLOCK):
        sl = slice(e0, e0 + EXPERT_BLOCK)
        hg = jnp.einsum('nd,edf->nef', t, w_gate[sl])
        hu = jnp.einsum('nd,edf->nef', t, w_up[sl])
        hw = jax.nn.silu(hg) * hu * combine[:, sl, None]
        routed = routed + jnp.einsum('nef,efd->nd', hw, w_down[sl])
    shared = (jax.nn.silu(t @ ws_gate) * (t @ ws_up)) @ ws_down
    return (routed + shared).reshape(B, S, D)

def setup_inputs(seed: int = 0) -> dict:
    key = jax.random.key(seed)
    ks = jax.random.split(key, 32)
    L, D = DEPTH, D_MODEL

    def nrm(k, shape, scale):
        return jax.random.normal(k, shape, dtype=jnp.float32) * scale

    def gain(k, shape):
        return 1.0 + 0.02 * jax.random.normal(k, shape, dtype=jnp.float32)

    offset = jax.random.randint(ks[2], (BATCH, 1), 0, 256, dtype=jnp.int32) * CHUNK
    positions = offset + jnp.arange(SEQ, dtype=jnp.int32)[None, :]
    return {
        "x": nrm(ks[0], (BATCH, SEQ, D), 1.0),
        "c": nrm(ks[1], (BATCH, D), 1.0),
        "positions": positions,
        "norm_mix_g": gain(ks[3], (L, D)),
        "norm_ffn_g": gain(ks[4], (L, D)),
        "w_ada": nrm(ks[5], (L, D, 6 * D), 0.5 * D ** -0.5),
        "b_ada": nrm(ks[6], (L, 6 * D), 0.02),
        "w_in": nrm(ks[7], (L, D, IN_COLS), D ** -0.5),
        "gm_ln_g": gain(ks[8], (L, GM_GROUPS, GM_CH)),
        "gm_ln_b": nrm(ks[9], (L, GM_GROUPS, GM_CH), 0.02),
        "gm_ws": nrm(ks[10], (L, GM_GROUPS, GM_BLOCK, GM_BLOCK), GM_BLOCK ** -0.5),
        "gm_bs": gain(ks[11], (L, GM_GROUPS, GM_BLOCK)),
        "q_a_g": gain(ks[12], (L, Q_LORA)),
        "w_q_up": nrm(ks[13], (L, Q_LORA, MLA_HEADS * QK_DIM), Q_LORA ** -0.5),
        "kv_a_g": gain(ks[14], (L, KV_LORA)),
        "w_kv_up": nrm(ks[15], (L, KV_LORA, MLA_HEADS * (QK_NOPE + V_DIM)), KV_LORA ** -0.5),
        "q_norm_g": gain(ks[16], (L, QK_DIM)),
        "k_norm_g": gain(ks[17], (L, QK_DIM)),
        "out_norm_g": gain(ks[18], (L, MIX_WIDTH)),
        "w_out": nrm(ks[19], (L, MIX_WIDTH, D), MIX_WIDTH ** -0.5),
        "w_router": nrm(ks[20], (L, D, N_EXPERTS), D ** -0.5),
        "router_bias": nrm(ks[21], (L, N_EXPERTS), 0.01),
        "w_exp_gate": nrm(ks[22], (L, N_EXPERTS, D, EXPERT_FF), D ** -0.5),
        "w_exp_up": nrm(ks[23], (L, N_EXPERTS, D, EXPERT_FF), D ** -0.5),
        "w_exp_down": nrm(ks[24], (L, N_EXPERTS, EXPERT_FF, D), EXPERT_FF ** -0.5),
        "w_sh_gate": nrm(ks[25], (L, D, SHARED_FF), D ** -0.5),
        "w_sh_up": nrm(ks[26], (L, D, SHARED_FF), D ** -0.5),
        "w_sh_down": nrm(ks[27], (L, SHARED_FF, D), SHARED_FF ** -0.5),
    }

def reference(x, c, positions, norm_mix_g, norm_ffn_g, w_ada, b_ada, w_in,
              gm_ln_g, gm_ln_b, gm_ws, gm_bs, q_a_g, w_q_up, kv_a_g, w_kv_up,
              q_norm_g, k_norm_g, out_norm_g, w_out, w_router, router_bias,
              w_exp_gate, w_exp_up, w_exp_down, w_sh_gate, w_sh_up, w_sh_down):
    cos, sin = rope_tables(positions)
    c_act = jax.nn.silu(c)
    o1 = 2 * GM_WIDTH
    o2 = o1 + Q_LORA
    o3 = o2 + KV_LORA
    for l in range(DEPTH):
        mod = c_act @ w_ada[l] + b_ada[l]
        sh1, sc1, g1, sh2, sc2, g2 = [m[:, None, :] for m in jnp.split(mod, 6, axis=-1)]
        h = rms_norm(x, norm_mix_g[l]) * (1.0 + sc1) + sh1
        proj = h @ w_in[l]
        gm_out = gmlp_mixer(proj[..., :o1], gm_ln_g[l], gm_ln_b[l], gm_ws[l], gm_bs[l])
        mla_out = mla_mixer(proj[..., o1:o2], proj[..., o2:o3], proj[..., o3:], cos, sin,
                            q_a_g[l], w_q_up[l], kv_a_g[l], w_kv_up[l], q_norm_g[l], k_norm_g[l])
        mixed = jnp.concatenate([rms_norm(gm_out, out_norm_g[l, :GM_WIDTH]),
                                 rms_norm(mla_out, out_norm_g[l, GM_WIDTH:])], axis=-1)
        x = x + g1 * (mixed @ w_out[l])
        h = rms_norm(x, norm_ffn_g[l]) * (1.0 + sc2) + sh2
        x = x + g2 * moe_ffn(h, w_router[l], router_bias[l], w_exp_gate[l], w_exp_up[l],
                             w_exp_down[l], w_sh_gate[l], w_sh_up[l], w_sh_down[l])
    return x


_drawn_inputs = setup_inputs


def setup_inputs(seed=0):
    import zlib

    import numpy as np

    out = dict(_drawn_inputs(seed))
    spreads = {}
    factors = {'norm_mix_g': 4.232,
     'gm_ln_g': 27.906,
     'gm_ln_b': 32.392,
     'gm_bs': 23.117,
     'q_a_g': 8.0,
     'kv_a_g': 4.703,
     'q_norm_g': 5.923,
     'k_norm_g': 8.0,
     'out_norm_g': 3.948,
     'norm_ffn_g': 2.926}
    for name, (base, spread) in spreads.items():
        noise = np.random.default_rng([zlib.crc32(name.encode()), seed]).standard_normal(out[name].shape)
        drawn = base * np.exp(spread * noise) if base else spread * noise
        out[name] = __import__('jax').numpy.asarray(drawn.astype(out[name].dtype))
    for name, factor in factors.items():
        out[name] = (out[name] * factor).astype(out[name].dtype)
    return out
```

```python
from contextlib import ExitStack

import numpy as np

import concourse.bass as bass
from concourse import mybir

F32 = mybir.dt.float32
I32 = mybir.dt.int32
ALU = mybir.AluOpType
ACT = mybir.ActivationFunctionType
AX = mybir.AxisListType

P = 128
KB = 1024
BIG = 8192.0
NEG = -1.0e30
EPS = 1e-6
CHUNK = 64
TOP_K = 8
N_GROUPS = 8
TOPK_GROUPS = 4
ROUTED_SCALE = 2.5
ROPE_THETA = 10000.0
TWO_PI = (6.28125, 0.00193500518798828125, float(2 * np.pi - 6.28125 - 0.00193500518798828125))
PI_BELOW = 3.1415925
MAGIC = 1.5 * 2.0 ** 23


def trunk_kernel(nc, a, out):
    S, D = a["x"].shape[1:]
    T = S // P
    C = D // P
    GW = a["gm_ln_g"].shape[1] * a["gm_ln_g"].shape[2]
    GG, GB = a["gm_ws"].shape[1:3]
    QL, KL = a["q_a_g"].shape[1], a["kv_a_g"].shape[1]
    QC, KC = QL // P, KL // P
    QD = a["q_norm_g"].shape[1]
    H = a["w_q_up"].shape[2] // QD
    KVD = a["w_kv_up"].shape[2] // H
    VD = (D - GW) // H
    NOPE = KVD - VD
    ROPE = QD - NOPE
    RH = ROPE // 2
    IN = a["w_in"].shape[2]
    LAT = IN - 2 * GW
    NE, _, FF = a["w_exp_gate"].shape[1:]
    FC = FF // P
    EG = NE // N_GROUPS
    BANK = 512
    ADA = a["w_ada"].shape[2] // BANK
    ADA_PE = 4
    MAXX = 32
    NSMALL = 9
    scale = float(QD) ** -0.5
    inv_freq = (1.0 / (np.float32(ROPE_THETA) ** (np.arange(0, ROPE, 2, dtype=np.float32) / np.float32(ROPE)))).astype(np.float32)

    h2_dram = nc.dram_tensor("h2_rows", [S, D], F32).ap()
    y8_dram = nc.dram_tensor("expert_rows", [S * TOP_K, D], F32).ap()

    with ExitStack() as ctx:
        SLAB = 207 * KB
        ctx.enter_context(nc.sbuf_tensor("slab", [P, SLAB // 4], F32))
        base = nc.sbuf_base - SLAB

        def at(name, kb, shape, dt=F32):
            return nc.alloc_sbuf_tensor_at(name, shape, dt, offset=base + int(kb * KB))

        def sem(name):
            return ctx.enter_context(nc.semaphore(name))

        bank = [ctx.enter_context(nc.psum_tensor(f"bank{i}", [P, BANK], F32)) for i in range(8)]

        x = at("x_sb", 0, [P, T, D])
        mod = at("mod_rows", 16, [P, 6, D])
        SH1, G1, GATE1, SH2, G2, GATE2 = range(6)
        w_in = at("w_in_sb", 40, [P, C, IN])
        ada_w = [at(f"ada_w{i}", 94 + 16 * i, [P, C, BANK]) for i in range(2)]
        h = at("h_sb", 126, [P, T, D])
        hT = at("hT", 143, [P, C, S])
        cbc = at("cbc", 159, [P, C, P])
        gmix = at("gmix", 163, [P, D])
        u = at("u_sb", 159, [P, T, GW])
        v = at("v_sb", 167, [P, T, GW])
        lat = at("lat_sb", 175, [P, T, LAT])
        w_q = at("w_q_sb", 126, [P, QC, H * QD])
        w_kv = at("w_kv_sb", 135, [P, KC, H * KVD])
        q = at("q_sb", 40, [P, T, H, QD])
        k = at("k_sb", 52, [P, T, H, QD])
        sq = at("sq_sb", 64, [P, 2, H, QD])
        rt = [at(f"rope_t{i}", 64 + 2 * i, [P, T, H, RH]) for i in range(4)]
        vv = at("vv_sb", 72, [P, T, H, VD])
        qT = at("qT", 80, [P, H, S])
        kT = at("kT", 96, [P, H, S])
        latT = at("latT", 112, [P, QC + KC, S])
        NPB = 3
        prob = [at(f"prob{i}", 112 + 2 * i, [P, S]) for i in range(NPB)]
        probT = [at(f"probT{i}", 118 + 2 * i, [P, S]) for i in range(NPB)]
        mixed = at("mixed", 143, [P, T, D])
        osq = at("osq", 130, [P, D])
        w_out = at("w_out_sb", 40, [P, C, D])
        mixT = at("mixT", 80, [P, C, S])
        h2 = at("h2_sb", 96, [P, T, D])
        h2T = at("h2T", 112, [P, C, S])
        w_r = at("w_r_sb", 128, [P, C, NE])
        xtmp = at("xtmp", 130, [P, D])
        gffn = at("gffn", 159, [P, D])
        ws_g = at("ws_g", 159, [P, C, FF])
        ws_u = at("ws_u", 167, [P, C, FF])
        ws_d = at("ws_d", 175, [P, FC, D])
        sco = at("sco", 151, [P, T, NE])
        bia = at("bia", 152, [P, T, NE])
        rep = at("rep", 153, [P, T, NE])
        m8 = at("m8", 154, [P, T * N_GROUPS, 8])
        cge = at("cge", 155, [P, T, N_GROUPS, N_GROUPS])
        cgt = at("cgt", 156, [P, T, N_GROUPS, N_GROUPS])
        rank = at("rank", 157, [P, T, NE])
        comb = at("comb", 158, [P, T, NE])
        gsum = at("gsum", 130, [P, T, N_GROUPS])
        gmask = at("gmask", 130.25, [P, T, N_GROUPS])
        gneg = at("gneg", 130.5, [P, T, N_GROUPS])
        grank = at("grank", 130.75, [P, T, N_GROUPS])
        v8 = at("v8", 131, [P, T, 8])
        wsum = at("wsum", 131.25, [P, T])
        zero = at("zero", 131.5, [P, 3 * NE])
        flag = at("flag", 132.25, [P, 3 * NE])
        runs = at("runs", 133, [P, 3 * NE])
        lcol = at("lcol", 151, [P, 2])
        lmat = at("lmat", 151.5, [P, 2, MAXX])
        ltmp = at("ltmp", 152, [P, 3 * NE])
        eblk = at("eblk", 153, [P, 2, 3, NE])
        w_gu = [at(f"w_gu{i}", 40 + 24 * i, [P, 2, C, FF]) for i in range(2)]
        w_d = [at(f"w_d{i}", 56 + 24 * i, [P, FC, D]) for i in range(2)]
        oute = [at(f"oute{i}", 88 + 4 * i, [P, D]) for i in range(2)]
        pay = at("pay", 96, [P, T, NE, 4])
        selm = at("selm", 100, [P, T, NE])
        posm = at("posm", 101, [P, T, NE])
        onehot = [at(f"onehot{i}", 134 + 2 * i, [P, T, P]) for i in range(2)]
        sgate = [at(f"sgate{i}", 138 + i, [P, FF]) for i in range(2)]
        hw = [at(f"hw{i}", 140 + i, [P, FF]) for i in range(2)]
        hwT = at("hwT", 142, [P, FC, P])
        xe = [at(f"xe{i}", 143 + 4 * i, [P, D]) for i in range(2)]
        xeT = [at(f"xeT{i}", 151 + 4 * i, [P, C, P]) for i in range(2)]
        yrows = [at(f"yrows{i}", 40 + 32 * i, [P, TOP_K, D]) for i in range(2)]
        place = [186.0]

        def small(name, shape, dt=F32):
            t = at(name, place[0], shape, dt)
            place[0] += -(-int(np.prod(shape[1:])) // 8) / 32
            assert place[0] <= 207, name
            return t

        ident = small("ident", [P, P])
        ones = small("ones", [P, P])
        tri = small("tri", [P, P])
        gtri = small("gtri", [P, N_GROUPS, N_GROUPS])
        iota = small("iota", [P, P])
        tok = small("tok", [P, T])
        part = small("part", [P, 1])
        epsc = small("epsc", [P, 1])
        freq = small("freq", [P, RH])
        cT = small("cT", [P, C])
        cact = small("cact", [P, C])
        b_ada = small("b_ada_rows", [P, BANK])
        acc = [small(f"ada_acc{i}", [P, BANK]) for i in range(2)]
        ss = small("ss", [P, T])
        lnst = small("lnst", [P, T * GG, 6])
        lnmv = small("lnmv", [P, T * GG, 2])
        latss = small("latss", [P, T, 2])
        qkss = small("qkss", [P, 2, T, H])
        oss = small("oss", [P, T, 2])
        ln_g = small("ln_g", [P, GW])
        ln_b = small("ln_b", [P, GW])
        ws_raw = small("ws_raw", [P, GG, GB])
        lsq = at("lsq", place[0], [P, QL])
        ws_low = small("ws_low", [P, GG, GB])
        bsT = small("bsT", [P, GG])
        qa_g = small("qa_g", [P, QC])
        kva_g = small("kva_g", [P, KC])
        qn_g = small("qn_g", [P, QD])
        kn_g = small("kn_g", [P, QD])
        on_g = small("on_g", [P, C])
        rbias = small("rbias", [P, NE])
        posi = small("posi", [P, T], I32)
        posf = small("posf", [P, T])
        ang = small("ang", [P, T, RH])
        turns = small("turns", [P, T, RH])
        cos = small("cos", [P, T, RH])
        sin = small("sin", [P, T, RH])
        den = small("den", [P, T, H])
        nmax = small("nmax", [P, T, H])
        src_i = [small(f"src_i{i}", [P, 2], I32) for i in range(4)]
        combw = [small(f"combw{i}", [P, 1]) for i in range(4)]
        list_i = small("list_i", [P, 2 * MAXX], I32)
        list_f = small("list_f", [P, 2 * MAXX])
        nextra = small("nextra", [P, 1], I32)
        cnt = small("cnt", [P, NE])
        posx = small("posx", [P, T])

        ld = {n: sem("ld_" + n) for n in ("x", "c", "bada", "pos", "gmix", "gffn", "small", "ws", "win", "wq", "wout", "wr", "wsh")}
        ld_ada = [sem("ld_ada0"), sem("ld_ada1")]
        (consts, dve_step, act_step, pool_step, silu_c, cbc_ok, ada_pe, ada_dve, acc_ok, ada_mm, mod_ok, g1_ok,
         g2_ok, ss_ok, std_ok, h_ok, hT_tr, hT_ok, wsT_tr, wsT_ok, proj_mm, proj_ok) = (sem(n) for n in (
            "consts", "dve_step", "act_step", "pool_step", "silu_c", "cbc_ok", "ada_pe", "ada_dve", "acc_ok", "ada_mm",
            "mod_ok", "g1_ok", "g2_ok", "ss_ok", "std_ok", "h_ok", "hT_tr", "hT_ok", "wsT_tr", "wsT_ok", "proj_mm", "proj_ok"))
        (stats_ok, lstd_ok, lrstd_ok, latn_ok, latT_tr, latT_ok, v_ok, gate_mm, gate_ok, kpe_ok, up_mm, up_ok, sq_ok,
         ssq_ok, qstd_ok, ang_ok, trig_ok, qk_ok, qkT_tr, qkT_ok) = (sem(n) for n in (
            "stats_ok", "lstd_ok", "lrstd_ok", "latn_ok", "latT_tr", "latT_ok", "v_ok", "gate_mm", "gate_ok", "kpe_ok",
            "up_mm", "up_ok", "sq_ok", "ssq_ok", "qstd_ok", "ang_ok", "trig_ok", "qk_ok", "qkT_tr", "qkT_ok"))
        (s_mm, nmax_ok, exp_ok, pT_tr, pT_ok, av_mm, o_ok, oss_ok, ostd_ok, orstd_ok, mix_ok, mixT_tr, mixT_ok, out_mm,
         x1_ok, ss2_ok, std2_ok, h2_ok, st_h2, h2T_tr, h2T_ok, rt_mm, sco_ok, selm_ok, pos_mm, pay_ok, lmat_ok, list_mm,
         list_ok) = (sem(n) for n in (
            "s_mm", "nmax_ok", "exp_ok", "pT_tr", "pT_ok", "av_mm", "o_ok", "oss_ok", "ostd_ok", "orstd_ok", "mix_ok",
            "mixT_tr", "mixT_ok", "out_mm", "x1_ok", "ss2_ok", "std2_ok", "h2_ok", "st_h2", "h2T_tr", "h2T_ok", "rt_mm",
            "sco_ok", "selm_ok", "pos_mm", "pay_ok", "lmat_ok", "list_mm", "list_ok"))
        (sgu_mm, ssilu_ok, shw_ok, shT_tr, shT_ok, sd_mm, sh_ok) = (sem(n) for n in (
            "sgu_mm", "ssilu_ok", "shw_ok", "shT_tr", "shT_ok", "sd_mm", "sh_ok"))
        ld_gu = [sem("ld_gu0"), sem("ld_gu1")]
        ld_d = [sem("ld_d0"), sem("ld_d1")]
        ld_xe = [sem("ld_xe0"), sem("ld_xe1")]
        st_y = [sem("st_y0"), sem("st_y1")]
        ld_y = [sem("ld_y0"), sem("ld_y1")]
        (oh_ok, idx_mm, idx_ok, xe_set, xeT_tr, xeT_a, xeT_v, gu_mm, silu_ok, hw_ok, hwT_tr, hwT_ok, d_mm, oute_a,
         oute_v, fin_ok, st_out, posx_ok) = (sem(n) for n in (
            "oh_ok", "idx_mm", "idx_ok", "xe_set", "xeT_tr", "xeT_a", "xeT_v", "gu_mm", "silu_ok", "hw_ok", "hwT_tr",
            "hwT_ok", "d_mm", "oute_a", "oute_v", "fin_ok", "st_out", "posx_ok"))

        def num(E, d=0):
            m, r = E
            return r + d if m is None else m * 4 + (r + d)

        def pairs(E, d=0):
            m, r = E
            return r // 2 + 1 + d if m is None else m * 2 + (r // 2 + 1 + d)

        def after(E, d):
            return E[0], E[1] + d

        def exists(E):
            return E[0] is not None or E[1] < NE

        def wait(eng, s, value):
            if not isinstance(value, int) or value > 0:
                eng.wait_ge(s, value)

        apart_sem = {"sp": sem("sp_apart"), "pool": sem("pool_apart")}

        def apart(eng, name):
            eng.sem_inc(apart_sem[name], 1)

        HEAD = 4

        def every_expert(eng, step):
            for r in range(HEAD):
                step((None, r))
            with eng.Fori(0, (NE - 2 * HEAD) // 4) as m:
                for r in range(4):
                    step((m, HEAD + r))
            for r in range(NE - HEAD, NE):
                step((None, r))

        def extra_blocks(eng, step):
            eng.wait_ge(list_ok, 2)
            n = eng.value_load(nextra[0:1, 0:1], min_val=0, max_val=MAXX)
            with eng.If(n > 0):
                with eng.Fori(0, n) as i:
                    step(i)
            return n

        x_dram = a["x"].rearrange("b (t p) d -> p (b t) d", p=P)
        out_dram = out.rearrange("b (t p) d -> p (b t) d", p=P)
        w_ada_v = a["w_ada"][0].rearrange("(p c) n -> p c n", c=C)

        def bcast(ap, n):
            return ap.rearrange("l n -> (l n)").unsqueeze(0).to_broadcast([P, n])

        cuts = [(n0, min(n0 + BANK, IN)) for n0 in range(0, IN, BANK)]
        NB = len(cuts)
        NI = T * H
        EXTRA0 = NE // 2

        block = ctx.enter_context(nc.Block())

        @block.sync
        def _(sp):
            sp.dma_start(cT[:], a["c"].rearrange("b (p c) -> p (b c)", c=C)).then_inc(ld["c"], 16)
            sp.dma_start(ada_w[0][:], w_ada_v[:, :, 0:BANK]).then_inc(ld_ada[0], 16)
            sp.dma_start(x[:], x_dram).then_inc(ld["x"], 16)
            sp.dma_start(ada_w[1][:], w_ada_v[:, :, BANK:2 * BANK]).then_inc(ld_ada[1], 16)
            for j in range(2, ADA):
                if j - 2 < ADA_PE:
                    sp.wait_ge(ada_pe, j - 1)
                else:
                    sp.wait_ge(ada_dve, j - 1 - ADA_PE)
                sp.dma_start(ada_w[j % 2][:], w_ada_v[:, :, j * BANK:(j + 1) * BANK]).then_inc(ld_ada[j % 2], 16)
                if j == ADA_PE - 1:
                    sp.dma_start(w_in[:], a["w_in"][0].rearrange("(p c) n -> p c n", c=C)).then_inc(ld["win"], 16)
            sp.wait_ge(hT_tr, 2 * T)
            sp.dma_start(w_q[:], a["w_q_up"][0].rearrange("(p c) n -> p c n", c=QC)).then_inc(ld["wq"], 16)
            sp.dma_start(w_kv[:], a["w_kv_up"][0].rearrange("(p c) n -> p c n", c=KC)).then_inc(ld["wq"], 16)
            sp.wait_ge(qkT_tr, 4 * T)
            sp.dma_start(w_out[:], a["w_out"][0].rearrange("(p c) n -> p c n", c=C)).then_inc(ld["wout"], 16)
            sp.wait_ge(gate_ok, GG)
            sp.dma_start(gffn[:], bcast(a["norm_ffn_g"], D)).then_inc(ld["gffn"], 16)
            sp.dma_start(w_r[:], a["w_router"][0].rearrange("(p c) n -> p c n", c=C)).then_inc(ld["wr"], 16)
            sp.wait_ge(kpe_ok, T)
            sp.wait_ge(latT_tr, QC + KC)
            sp.dma_start(ws_u[:], a["w_sh_up"][0].rearrange("(p c) n -> p c n", c=C)).then_inc(ld["wsh"], 16)
            sp.dma_start(ws_d[:], a["w_sh_down"][0].rearrange("(p c) n -> p c n", c=FC)).then_inc(ld["wsh"], 16)
            sp.wait_ge(g2_ok, 1)
            sp.dma_start(ws_g[:], a["w_sh_gate"][0].rearrange("(p c) n -> p c n", c=C)).then_inc(ld["wsh"], 16)

            def load_expert(e, i):
                for m, w in enumerate(("w_exp_gate", "w_exp_up")):
                    sp.dma_start(w_gu[i][:, m], a[w][0, bass.ds(e, 1)].rearrange("o (p c) n -> p (o c) n", c=C)).then_inc(ld_gu[i], 16)

            def load_down(e, i):
                sp.dma_start(w_d[i][:], a["w_exp_down"][0, bass.ds(e, 1)].rearrange("o (p c) n -> p (o c) n", c=FC)).then_inc(ld_d[i], 16)

            def step(E):
                i = E[1] % 2
                wait(sp, gu_mm, num(E, -1))
                apart(sp, "sp")
                load_expert(num(E), i)
                wait(sp, d_mm, num(E, -1))
                apart(sp, "sp")
                load_down(num(E), i)
                if E[0] is None and E[1] == 1:
                    for t in range(T):
                        sp.wait_ge(h2_ok, t + 1)
                        sp.dma_start(h2_dram[t * P:(t + 1) * P, :], h2[:, t]).then_inc(st_h2, 16)

            sp.wait_ge(out_mm, 2 * T)
            every_expert(sp, step)

            def extra(i):
                e = sp.value_load(list_i[0:1, bass.ds(i, 1)], min_val=0, max_val=NE - 1)
                sp.wait_ge(d_mm, i + NE)
                apart(sp, "sp")
                load_expert(e, 0)
                load_down(e, 0)

            n = extra_blocks(sp, extra)
            sp.wait_ge(st_y[0], n * 16 + 16 * EXTRA0)
            apart(sp, "sp")
            sp.wait_ge(st_y[1], 16 * (NE - EXTRA0))
            sp.wait_ge(d_mm, n + NE)
            sp.wait_ge(st_h2, 16 * T)
            for t in range(T):
                if t >= 2:
                    sp.wait_ge(fin_ok, t - 1)
                    sp.dma_start(out_dram[:, t - 2], x[:, t - 2]).then_inc(st_out, 16)
                sp.dma_start(yrows[t % 2][:], y8_dram[t * P * TOP_K:(t + 1) * P * TOP_K, :].rearrange("(p j) d -> p j d", j=TOP_K)).then_inc(ld_y[t % 2], 16)
            for t in range(T - 2, T):
                sp.wait_ge(fin_ok, t + 1)
                sp.dma_start(out_dram[:, t], x[:, t]).then_inc(st_out, 16)
            sp.wait_ge(st_out, 16 * T)

        @block.gpsimd
        def _(pool):
            pool.memset(ones[:], 1.0).then_inc(consts, 1)
            pool.memset(epsc[:], EPS).then_inc(consts, 1)
            pool.wait_ge(consts, 2)
            pool.affine_select(out=ident[:], in_=ones[:], compare_op=ALU.is_equal, fill=0.0, base=0, pattern=[[-1, P]], channel_multiplier=1).then_inc(consts, 1)
            pool.iota(tok[:], pattern=[[P, T]], base=0, channel_multiplier=1, allow_small_or_imprecise_dtypes=True).then_inc(consts, 1)
            for i in range(RH):
                last = pool.memset(freq[:, i:i + 1], float(inv_freq[i]))
            last.then_inc(consts, 1)
            pool.affine_select(out=tri[:], in_=ones[:], compare_op=ALU.is_gt, fill=0.0, base=0, pattern=[[1, P]], channel_multiplier=-1).then_inc(consts, 1)
            pool.affine_select(out=gtri[:], in_=ones[:, 0:N_GROUPS ** 2].rearrange("p (a b) -> p a b", a=N_GROUPS), compare_op=ALU.is_gt, fill=0.0, base=0,
                               pattern=[[1, N_GROUPS], [-1, N_GROUPS]], channel_multiplier=0).then_inc(consts, 1)
            pool.iota(iota[:], pattern=[[1, P]], base=0, channel_multiplier=0, allow_small_or_imprecise_dtypes=True).then_inc(consts, 1)
            pool.iota(part[:], pattern=[[0, 1]], base=0, channel_multiplier=1, allow_small_or_imprecise_dtypes=True).then_inc(consts, 1)
            pool.wait_ge(ld["ws"], 16)
            pool.affine_select(out=ws_low[:], in_=ws_raw[:], compare_op=ALU.is_ge, fill=0.0, base=0, pattern=[[0, GG], [-1, GB]], channel_multiplier=1).then_inc(consts, 1)
            for t in range(T):
                pool.wait_ge(proj_ok, (t + 1) * NB)
                if t == 0:
                    pool.wait_ge(proj_mm, T * NB)
                pool.tensor_copy(k[:, t, :, NOPE:QD], lat[:, t, QL + KL:LAT].unsqueeze(1).to_broadcast([P, H, ROPE])).then_inc(kpe_ok, 1)

            pool.wait_ge(mixT_tr, C)
            for i in range(2):
                pool.memset(xe[i][:], 0.0).then_inc(xe_set, 1)
            pool.wait_ge(selm_ok, 1)
            pool.iota(eblk[:, 0], pattern=[[0, 3], [1, NE]], base=0, channel_multiplier=0, allow_small_or_imprecise_dtypes=True)
            pool.iota(eblk[:, 1], pattern=[[P, 3], [0, NE]], base=P, channel_multiplier=0, allow_small_or_imprecise_dtypes=True).then_inc(pool_step, 1)
            pool.wait_ge(st_h2, 16 * T)

            last_row = pool.to_reg(S - 1)
            last_result = pool.to_reg(S * TOP_K - 1)

            def gather(j, i):
                apart(pool, "pool")
                pool.indirect_dma_start(xe[i][:], None, h2_dram, bass.IndirectOffsetOnAxis(ap=src_i[j][:, 0:1], axis=0),
                                        bounds_check=last_row, oob_is_err=False).then_inc(ld_xe[i], 16)

            def scatter(j, i):
                apart(pool, "pool")
                pool.indirect_dma_start(y8_dram, bass.IndirectOffsetOnAxis(ap=src_i[j][:, 1:2], axis=0), oute[i][:], None,
                                        bounds_check=last_result, oob_is_err=False).then_inc(st_y[i], 16)

            pool.wait_ge(xe_set, 2)
            for r in range(3):
                pool.wait_ge(idx_ok, r + 1)
                if r == 2:
                    pool.wait_ge(xeT_tr, 1)
                gather(r % 4, r % 2)

            def step(E):
                G = after(E, 3)
                if exists(G):
                    pool.wait_ge(idx_ok, num(G, 1))
                    pool.wait_ge(xeT_tr, num(G, -1))
                    gather(G[1] % 4, G[1] % 2)
                pool.wait_ge(oute_a, num(E, 1))
                pool.wait_ge(oute_v, num(E, 1))
                scatter(E[1] % 4, E[1] % 2)

            every_expert(pool, step)

            def extra(i):
                pool.wait_ge(idx_ok, i + (NE + 1))
                gather(0, 0)
                pool.wait_ge(oute_a, i + (NE + 1))
                pool.wait_ge(oute_v, i + (NE + 1))
                scatter(0, 0)

            extra_blocks(pool, extra)

        @block.tensor
        def _(pe):
            def bias_row(j):
                pe.matmul(bank[j % 2][:], ident[0:ADA, j:j + 1].to_broadcast([ADA, P]), b_ada[0:ADA, :], start=False, stop=True).then_inc(ada_mm, 1)

            pe.wait_ge(consts, 3)
            pe.wait_ge(cbc_ok, 1)
            pe.wait_ge(ld["bada"], 16)
            for j in range(ADA_PE):
                pe.wait_ge(ld_ada[j % 2], 16 * (j // 2 + 1))
                if j >= 2:
                    pe.wait_ge(mod_ok, j - 1)
                for c in range(C):
                    last = pe.matmul(bank[j % 2][:], cbc[:, c, :], ada_w[j % 2][:, c, :], start=(c == 0), stop=False)
                last.then_inc(ada_pe, 1)
                bias_row(j)
            pe.wait_ge(consts, 10)
            for g in range(GG):
                last = pe.transpose(bank[2][:, g * GB:(g + 1) * GB], ws_low[:, g, :], ident[:])
            last.then_inc(wsT_tr, 1)
            for t in range(T):
                pe.wait_ge(h_ok, t + 1)
                for half in range(2):
                    i = 2 * t + half
                    if i >= 4:
                        pe.wait_ge(hT_ok, i - 3)
                    for c4 in range(4):
                        last = pe.transpose(bank[4 + i % 4][:, c4 * P:(c4 + 1) * P], h[:, t, half * 4 + c4::C], ident[:])
                    last.then_inc(hT_tr, 1)
            pe.wait_ge(ld["win"], 16)
            pe.wait_ge(hT_ok, 2 * T)
            pe.wait_ge(wsT_ok, 1)
            for t in range(T):
                for m, (n0, n1) in enumerate(cuts):
                    i = t * NB + m
                    b = 2 + i % 6
                    if i >= 6:
                        pe.wait_ge(proj_ok, i - 5)
                    for c in range(C):
                        last = pe.matmul(bank[b][:, 0:n1 - n0], hT[:, c, t * P:(t + 1) * P], w_in[:, c, n0:n1], start=(c == 0), stop=(c == C - 1))
                    last.then_inc(proj_mm, 1)
                for j in (ADA_PE + 2 * t, ADA_PE + 2 * t + 1):
                    pe.wait_ge(acc_ok, j - ADA_PE + 1)
                    pe.wait_ge(mod_ok, j - 1)
                    pe.matmul(bank[j % 2][:], ones[:], acc[j % 2][:], start=True, stop=False)
                    bias_row(j)
            pe.wait_ge(latn_ok, 1)
            pe.wait_ge(proj_ok, T * NB)
            for c in range(QC + KC):
                for t in range(T):
                    src = lat[:, t, c:QL:QC] if c < QC else lat[:, t, QL + c - QC:QL + KL:KC]
                    last = pe.transpose(bank[2 + c][:, t * P:(t + 1) * P], src, ident[:])
                last.then_inc(latT_tr, 1)
            pe.wait_ge(v_ok, 1)
            pe.wait_ge(mod_ok, ADA)
            for g in range(GG):
                if g == 3:
                    pe.wait_ge(gate_ok, 1)
                pe.matmul(bank[(7, 0, 1, 7)[g]][:], ws_raw[:, g, :], v[:, :, g * P:(g + 1) * P], start=True, stop=True).then_inc(gate_mm, 1)
            pe.wait_ge(ld["wq"], 32)
            pe.wait_ge(latT_ok, QC + KC)
            pe.wait_ge(gate_ok, GG)
            HQ, HK = H // 2 * QD, H // 2 * KVD
            for t in range(T):
                for m in range(4):
                    i = 4 * t + m
                    if i >= 8:
                        pe.wait_ge(up_ok, i - 7)
                    w, c0, cn, n0, n1 = (w_q, 0, QC, m * HQ, (m + 1) * HQ) if m < 2 else (w_kv, QC, KC, (m - 2) * HK, (m - 1) * HK)
                    for c in range(cn):
                        last = pe.matmul(bank[i % 8][:, 0:n1 - n0], latT[:, c0 + c, t * P:(t + 1) * P], w[:, c, n0:n1], start=(c == 0), stop=(c == cn - 1))
                    last.then_inc(up_mm, 1)
            pe.wait_ge(up_ok, 4 * T)
            for s, src in enumerate((q, k)):
                pe.wait_ge(qk_ok, s + 1)
                for t in range(T):
                    for half in range(2):
                        i = s * 2 * T + 2 * t + half
                        if i >= 8:
                            pe.wait_ge(qkT_ok, i - 7)
                        for hh in range(4):
                            last = pe.transpose(bank[i % 8][0:QD, hh * P:(hh + 1) * P], src[:, t, half * 4 + hh, :], ident[:])
                        last.then_inc(qkT_tr, 1)
            pe.wait_ge(qkT_ok, 4 * T)

            def scores(i):
                t, hd = divmod(i, H)
                if i >= 3:
                    pe.wait_ge(exp_ok, i - 2)
                pe.matmul(bank[i % 3][:, 0:(t + 1) * P], qT[0:QD, hd, t * P:(t + 1) * P], kT[0:QD, hd, 0:(t + 1) * P], start=True, stop=True).then_inc(s_mm, 1)

            def prob_transposes(i):
                t, hd = divmod(i, H)
                pe.wait_ge(exp_ok, i + 1)
                if i >= 3:
                    pe.wait_ge(pT_ok, i - 2)
                for kb in range(t + 1):
                    last = pe.transpose(bank[3 + i % 3][:, kb * P:(kb + 1) * P], prob[i % NPB][:, kb * P:(kb + 1) * P], ident[:])
                last.then_inc(pT_tr, 1)

            def weighted_values(i):
                t, hd = divmod(i, H)
                pe.wait_ge(pT_ok, i + 1)
                if hd == 0 and t >= 2:
                    pe.wait_ge(o_ok, t - 1)
                for kb in range(t + 1):
                    last = pe.matmul(bank[6 + t % 2][:, hd * VD:(hd + 1) * VD], probT[i % NPB][:, kb * P:(kb + 1) * P], vv[:, kb, hd, :], start=(kb == 0), stop=(kb == t))
                last.then_inc(av_mm, 1)

            scores(0)
            scores(1)
            prob_transposes(0)
            for i in range(NI):
                if i + 2 < NI:
                    scores(i + 2)
                if i + 1 < NI:
                    prob_transposes(i + 1)
                weighted_values(i)
            pe.wait_ge(mix_ok, 1)
            for c in range(C):
                if c >= 6:
                    pe.wait_ge(mixT_ok, c - 5)
                for t in range(T):
                    last = pe.transpose(bank[c % 6][:, t * P:(t + 1) * P], mixed[:, t, c::C], ident[:])
                last.then_inc(mixT_tr, 1)
            pe.wait_ge(ld["wout"], 16)
            pe.wait_ge(mixT_ok, C)
            for t in range(T):
                for m in range(2):
                    i = 2 * t + m
                    if i >= 4:
                        pe.wait_ge(x1_ok, i - 3)
                    for c in range(C):
                        last = pe.matmul(bank[i % 4][:], mixT[:, c, t * P:(t + 1) * P], w_out[:, c, m * BANK:(m + 1) * BANK], start=(c == 0), stop=(c == C - 1))
                    last.then_inc(out_mm, 1)
            for t in range(T):
                pe.wait_ge(h2_ok, t + 1)
                for half in range(2):
                    i = 2 * t + half
                    if i >= 2:
                        pe.wait_ge(h2T_ok, i - 1)
                    for c4 in range(4):
                        last = pe.transpose(bank[4 + i % 2][:, c4 * P:(c4 + 1) * P], h2[:, t, half * 4 + c4::C], ident[:])
                    last.then_inc(h2T_tr, 1)
            pe.wait_ge(ld["wr"], 16)
            pe.wait_ge(h2T_ok, 2 * T)
            for t in range(T):
                for c in range(C):
                    last = pe.matmul(bank[6][:, t * NE:(t + 1) * NE], h2T[:, c, t * P:(t + 1) * P], w_r[:, c, :], start=(c == 0), stop=(c == C - 1))
            last.then_inc(rt_mm, 1)

            def shared_gu(t):
                if t >= 2:
                    pe.wait_ge(shw_ok, t - 1)
                for m, w in enumerate((ws_g, ws_u)):
                    for c in range(C):
                        last = pe.matmul(bank[t % 2][:, m * FF:(m + 1) * FF], h2T[:, c, t * P:(t + 1) * P], w[:, c, :], start=(c == 0), stop=(c == C - 1))
                last.then_inc(sgu_mm, 1)

            def shared_hT(t):
                pe.wait_ge(shw_ok, t + 1)
                for j in range(FC):
                    last = pe.transpose(bank[7][:, j * P:(j + 1) * P], hw[t % 2][:, j::FC], ident[:])
                last.then_inc(shT_tr, 1)

            def shared_down(t):
                pe.wait_ge(shT_ok, t + 1)
                if t:
                    pe.wait_ge(sh_ok, t)
                for m in range(2):
                    for j in range(FC):
                        last = pe.matmul(bank[2 + m][:], hwT[:, j, :], ws_d[:, j, m * BANK:(m + 1) * BANK], start=(j == 0), stop=(j == FC - 1))
                last.then_inc(sd_mm, 1)

            pe.wait_ge(ld["wsh"], 48)
            pe.wait_ge(x1_ok, 2 * T)
            shared_gu(0)
            shared_gu(1)
            pe.wait_ge(selm_ok, 1)
            pe.wait_ge(sco_ok, 1)
            for t in range(T):
                for t2 in range(t + 1):
                    pe.matmul(bank[6][:, t * NE:(t + 1) * NE], tri[:] if t2 == t else ones[:], selm[:, t2, :], start=(t2 == 0), stop=(t2 == t))
            for t in range(T):
                last = pe.matmul(bank[6][:, T * NE:(T + 1) * NE], ones[:], selm[:, t, :], start=(t == 0), stop=(t == T - 1))
            last.then_inc(pos_mm, 1)

            def indices(i, e, n):
                pe.wait_ge(oh_ok, n + 1)
                wait(pe, idx_ok, n)
                for t in range(T):
                    last = pe.matmul(bank[6][:, 0:4], onehot[i][:, t, :], pay[:, t, bass.ds(e, 1), :].rearrange("p o c -> p (o c)"), start=(t == 0), stop=(t == T - 1))
                last.then_inc(idx_mm, 1)

            def rows_T(i, loads, n):
                pe.wait_ge(ld_xe[i], loads)
                wait(pe, xeT_a, n)
                wait(pe, xeT_v, n)
                for c in range(C):
                    last = pe.transpose(bank[c // 4][:, c % 4 * P:(c % 4 + 1) * P], xe[i][:, c::C], ident[:])
                last.then_inc(xeT_tr, 1)

            def gate_up(i, loads, n, before):
                pe.wait_ge(ld_gu[i], loads)
                pe.wait_ge(xeT_a, n + 1)
                pe.wait_ge(xeT_v, n + 1)
                wait(pe, hw_ok, before)
                for c in range(C):
                    last = pe.matmul(bank[2 + i][:], xeT[i][:, c, :], w_gu[i][:, :, c, :], start=(c == 0), stop=(c == C - 1))
                last.then_inc(gu_mm, 1)

            def hidden_T(i, n):
                pe.wait_ge(hw_ok, n + 1)
                wait(pe, hwT_ok, n)
                for j in range(FC):
                    last = pe.transpose(bank[7][:, j * P:(j + 1) * P], hw[i][:, j::FC], ident[:])
                last.then_inc(hwT_tr, 1)

            def down(i, loads, n):
                pe.wait_ge(ld_d[i], loads)
                pe.wait_ge(hwT_ok, n + 1)
                wait(pe, oute_a, n)
                wait(pe, oute_v, n)
                for m in range(2):
                    for j in range(FC):
                        last = pe.matmul(bank[4 + m][:], hwT[:, j, :], w_d[i][:, j, m * BANK:(m + 1) * BANK], start=(j == 0), stop=(j == FC - 1))
                last.then_inc(d_mm, 1)

            def rows_T_of(E):
                rows_T(E[1] % 2, times16(pairs(E)), num(E))

            def gate_up_of(E):
                gate_up(E[1] % 2, times16(pairs(E), 32), num(E), num(E, -1))

            shared_hT(0)
            pe.wait_ge(pay_ok, 1)
            for r in range(3):
                indices(r % 2, r, r)
            pe.wait_ge(lmat_ok, 1)
            pe.wait_ge(idx_ok, 3)
            pe.matmul(bank[6][:, 0:2 * MAXX], ones[0:MAXX, :], lmat[0:MAXX], start=True, stop=True).then_inc(list_mm, 1)
            for t in range(T):
                if t:
                    shared_hT(t)
                shared_down(t)
                if t + 2 < T:
                    shared_gu(t + 2)
            pe.wait_ge(list_ok, 2)
            pe.wait_ge(sh_ok, T)
            rows_T_of((None, 0))
            gate_up_of((None, 0))
            rows_T_of((None, 1))

            def step(E):
                if exists(after(E, 1)):
                    gate_up_of(after(E, 1))
                hidden_T(E[1] % 2, num(E))
                if exists(after(E, 3)):
                    indices((E[1] + 3) % 2, num(E, 3), num(E, 3))
                if exists(after(E, 2)):
                    rows_T_of(after(E, 2))
                down(E[1] % 2, times16(pairs(E)), num(E))

            every_expert(pe, step)

            def extra(i):
                e = pe.value_load(list_i[0:1, bass.ds(i, 1)], min_val=0, max_val=NE - 1)
                n = i + NE
                indices(0, e, n)
                rows_T(0, i * 16 + 16 * (EXTRA0 + 1), n)
                gate_up(0, i * 32 + 32 * (EXTRA0 + 1), n, n)
                hidden_T(0, n)
                down(0, i * 16 + 16 * (EXTRA0 + 1), n)

            extra_blocks(pe, extra)

        @block.scalar
        def _(act):
            act.dma_start(b_ada[0:ADA, :], a["b_ada"].rearrange("l (j n) -> (l j) n", n=BANK)).then_inc(ld["bada"], 16)
            act.dma_start(posi[:], a["positions"].rearrange("b (t p) -> p (b t)", p=P), allow_slow_non_contiguous=True).then_inc(ld["pos"], 16)
            act.dma_start(gmix[:], bcast(a["norm_mix_g"], D)).then_inc(ld["gmix"], 16)
            act.dma_start(ws_raw[:], a["gm_ws"].rearrange("l g t s -> t (l g) s")).then_inc(ld["ws"], 16)
            smalls = [
                (ln_g[:], bcast(a["gm_ln_g"].rearrange("l g c -> l (g c)"), GW)),
                (ln_b[:], bcast(a["gm_ln_b"].rearrange("l g c -> l (g c)"), GW)),
                (bsT[:], a["gm_bs"].rearrange("l g t -> t (l g)")),
                (qa_g[:], a["q_a_g"].rearrange("l (p c) -> p (l c)", c=QC)),
                (kva_g[:], a["kv_a_g"].rearrange("l (p c) -> p (l c)", c=KC)),
                (qn_g[:], bcast(a["q_norm_g"], QD)),
                (kn_g[:], bcast(a["k_norm_g"], QD)),
                (on_g[:], a["out_norm_g"].rearrange("l (p c) -> p (l c)", c=C)),
                (rbias[:], bcast(a["router_bias"], NE)),
            ]
            assert len(smalls) == NSMALL
            for dst, src in smalls:
                act.dma_start(dst, src, allow_slow_non_contiguous=True).then_inc(ld["small"], 16)
            act.wait_ge(ld["c"], 16)
            act.activation(cact[:], cT[:], ACT.Silu).then_inc(silu_c, 1)
            act.wait_ge(ang_ok, 1)
            act.activation(sin[:], ang[:], ACT.Sin).then_inc(trig_ok, 1)
            act.activation(cos[:], turns[:], ACT.Sin).then_inc(trig_ok, 1)

            def copy_mod(j):
                act.wait_ge(ada_mm, j + 1)
                act.copy(mod[:, j // 2, j % 2 * BANK:(j % 2 + 1) * BANK], bank[j % 2][:]).then_inc(mod_ok, 1)

            act.wait_ge(ss_ok, 1)
            act.wait_ge(consts, 2)
            act.activation(ss[:], ss[:], ACT.Sqrt, bias=epsc[:], scale=1.0 / D).then_inc(std_ok, 1)
            for j in range(ADA_PE):
                copy_mod(j)
            for i in range(2 * T):
                t, half = divmod(i, 2)
                act.wait_ge(hT_tr, i + 1)
                act.copy(hT[:, half * 4:half * 4 + 4, t * P:(t + 1) * P], bank[4 + i % 4][:].rearrange("p (c n) -> p c n", c=4)).then_inc(hT_ok, 1)
            act.wait_ge(cbc_ok, 1)
            act.wait_ge(ada_mm, ADA_PE)
            act.wait_ge(g1_ok, 1)
            for t in range(T):
                for m, (n0, n1) in enumerate(cuts):
                    i = t * NB + m
                    act.wait_ge(proj_mm, i + 1)
                    src = bank[2 + i % 6][:, 0:n1 - n0]
                    if m < 2:
                        act.activation((u, v)[m][:, t, :], src, ACT.Gelu).then_inc(proj_ok, 1)
                    else:
                        act.copy(lat[:, t, n0 - 2 * GW:n1 - 2 * GW], src).then_inc(proj_ok, 1)
                copy_mod(ADA_PE + 2 * t)
                copy_mod(ADA_PE + 2 * t + 1)
            act.wait_ge(stats_ok, 1)
            act.activation(lnmv[:, :, 1], lnmv[:, :, 1], ACT.Sqrt, bias=epsc[:]).then_inc(lstd_ok, 1)
            act.activation(latss[:, :, 0], latss[:, :, 0], ACT.Sqrt, bias=epsc[:], scale=1.0 / QL).then_inc(lstd_ok, 1)
            act.activation(latss[:, :, 1], latss[:, :, 1], ACT.Sqrt, bias=epsc[:], scale=1.0 / KL).then_inc(lstd_ok, 1)
            act.wait_ge(lrstd_ok, 1)
            for t in range(T):
                for s, (n0, n1) in enumerate(((0, QL), (QL, QL + KL))):
                    last = act.activation(lat[:, t, n0:n1], lat[:, t, n0:n1], ACT.Copy, scale=latss[:, t, s:s + 1])
            last.then_inc(latn_ok, 1)
            for c in range(QC + KC):
                act.wait_ge(latT_tr, c + 1)
                gain = qa_g[:, c:c + 1] if c < QC else kva_g[:, c - QC:c - QC + 1]
                if c == 0:
                    act.wait_ge(ld["small"], 16 * NSMALL)
                    act.wait_ge(ada_dve, ADA - ADA_PE)
                act.activation(latT[:, c, :], bank[2 + c][:], ACT.Copy, scale=gain).then_inc(latT_ok, 1)
            act.wait_ge(kpe_ok, T)
            HH = H // 2
            for t in range(T):
                for m in range(4):
                    i = 4 * t + m
                    act.wait_ge(up_mm, i + 1)
                    if m < 2:
                        act.copy(q[:, t, m * HH:(m + 1) * HH, :], bank[i % 8][:, 0:HH * QD].rearrange("p (h d) -> p h d", h=HH)).then_inc(up_ok, 1)
                    else:
                        src = bank[i % 8][:].rearrange("p (h d) -> p h d", h=HH)
                        act.copy(k[:, t, (m - 2) * HH:(m - 1) * HH, 0:NOPE], src[:, :, 0:NOPE])
                        act.copy(vv[:, t, (m - 2) * HH:(m - 1) * HH, :], src[:, :, NOPE:KVD]).then_inc(up_ok, 1)
                for s, z in enumerate((q, k)):
                    if t:
                        act.wait_ge(ssq_ok, 2 * (t - 1) + s + 1)
                    act.wait_ge(up_ok, 4 * t + 2 * s + 2)
                    act.activation(sq[:, s], z[:, t], ACT.Square).then_inc(sq_ok, 1)
            act.wait_ge(ssq_ok, 2 * T)
            act.activation(qkss[:], qkss[:], ACT.Sqrt, bias=epsc[:], scale=1.0 / QD).then_inc(qstd_ok, 1)
            for i in range(4 * T):
                s, r = divmod(i, 2 * T)
                t, half = divmod(r, 2)
                act.wait_ge(qkT_tr, i + 1)
                act.copy((qT, kT)[s][0:QD, half * 4:half * 4 + 4, t * P:(t + 1) * P], bank[i % 8][0:QD, :].rearrange("p (h n) -> p h n", h=4)).then_inc(qkT_ok, 1)
            def exponential(i):
                t, hd = divmod(i, H)
                act.wait_ge(nmax_ok, i + 1)
                if i == 0:
                    act.wait_ge(up_mm, 4 * T)
                if i >= NPB:
                    act.wait_ge(pT_tr, i - NPB + 1)
                act.activation(prob[i % NPB][:, 0:(t + 1) * P], bank[i % 3][:, 0:(t + 1) * P], ACT.Exp, bias=nmax[:, t, hd:hd + 1],
                               accum_out=den[:, t, hd:hd + 1]).then_inc(exp_ok, 1)

            def prob_copy(i):
                t, hd = divmod(i, H)
                act.wait_ge(pT_tr, i + 1)
                if i >= NPB:
                    act.wait_ge(av_mm, i - NPB + 1)
                act.copy(probT[i % NPB][:, 0:(t + 1) * P], bank[3 + i % 3][:, 0:(t + 1) * P]).then_inc(pT_ok, 1)

            exponential(0)
            for i in range(NI):
                if i + 1 < NI:
                    exponential(i + 1)
                prob_copy(i)
            act.wait_ge(oss_ok, 1)
            act.activation(oss[:], oss[:], ACT.Sqrt, bias=epsc[:], scale=1.0 / GW).then_inc(ostd_ok, 1)
            act.wait_ge(orstd_ok, 1)
            for t in range(T):
                for s in range(2):
                    last = act.activation(mixed[:, t, s * GW:(s + 1) * GW], mixed[:, t, s * GW:(s + 1) * GW], ACT.Copy, scale=oss[:, t, s:s + 1])
            last.then_inc(mix_ok, 1)
            for c in range(C):
                act.wait_ge(mixT_tr, c + 1)
                act.activation(mixT[:, c, :], bank[c % 6][:], ACT.Copy, scale=on_g[:, c:c + 1]).then_inc(mixT_ok, 1)
            def std2(t):
                act.wait_ge(ss2_ok, t + 1)
                act.activation(ss[:, t:t + 1], ss[:, t:t + 1], ACT.Sqrt, bias=epsc[:], scale=1.0 / D).then_inc(std2_ok, 1)

            std2(0)
            for t in range(T):
                if t + 1 < T:
                    std2(t + 1)
                for half in range(2):
                    i = 2 * t + half
                    act.wait_ge(h2T_tr, i + 1)
                    act.copy(h2T[:, half * 4:half * 4 + 4, t * P:(t + 1) * P], bank[4 + i % 2][:].rearrange("p (c n) -> p c n", c=4)).then_inc(h2T_ok, 1)
            act.wait_ge(rt_mm, 1)
            act.activation(sco[:], bank[6][:, 0:T * NE].rearrange("p (t e) -> p t e", t=T), ACT.Sigmoid).then_inc(sco_ok, 1)
            def shared_silu(t):
                act.wait_ge(sgu_mm, t + 1)
                if t >= 2:
                    act.wait_ge(shw_ok, t - 1)
                act.activation(sgate[t % 2][:], bank[t % 2][:, 0:FF], ACT.Silu).then_inc(ssilu_ok, 1)

            def shared_hT_copy(t):
                act.wait_ge(shT_tr, t + 1)
                if t:
                    act.wait_ge(sd_mm, t)
                act.copy(hwT[:], bank[7][:, 0:FC * P].rearrange("p (j n) -> p j n", j=FC)).then_inc(shT_ok, 1)

            shared_silu(0)
            shared_silu(1)
            for t in range(T):
                shared_hT_copy(t)
                if t + 2 < T:
                    shared_silu(t + 2)

            def rows_copy(i, n):
                act.wait_ge(xeT_tr, n + 1)
                act.copy(xeT[i][:, 0:4, :], bank[0][:].rearrange("p (c n) -> p c n", c=4)).then_inc(xeT_a, 1)

            def silu(i, n, free):
                act.wait_ge(gu_mm, n + 1)
                wait(act, hw_ok, free)
                act.activation(sgate[i][:], bank[2 + i][:, 0:FF], ACT.Silu).then_inc(silu_ok, 1)

            def hidden_copy(n):
                act.wait_ge(hwT_tr, n + 1)
                wait(act, d_mm, n)
                act.copy(hwT[:], bank[7][:, 0:FC * P].rearrange("p (j n) -> p j n", j=FC)).then_inc(hwT_ok, 1)

            def out_copy(i, n, stores):
                act.wait_ge(d_mm, n + 1)
                wait(act, st_y[i], stores)
                act.copy(oute[i][:, 0:BANK], bank[4][:]).then_inc(oute_a, 1)

            def rows_copy_of(E):
                if not (E[0] is None and E[1] < 2):
                    act.wait_ge(gu_mm, num(E, -1))
                rows_copy(E[1] % 2, num(E))

            act.wait_ge(pay_ok, 1)
            act.wait_ge(list_ok, 2)
            act.wait_ge(shw_ok, T)
            act.wait_ge(sd_mm, T)
            rows_copy_of((None, 0))
            silu(0, 0, 0)
            rows_copy_of((None, 1))

            def step(E):
                E1, E2 = after(E, 1), after(E, 2)
                if exists(E1):
                    silu(E1[1] % 2, num(E1), num(E1, -1))
                hidden_copy(num(E))
                if exists(E2):
                    rows_copy_of(E2)
                out_copy(E[1] % 2, num(E), times16(pairs(E, -1)))

            every_expert(act, step)

            def extra(i):
                n = i + NE
                rows_copy(0, n)
                silu(0, n, n)
                hidden_copy(n)
                out_copy(0, n, i * 16 + 16 * EXTRA0)

            extra_blocks(act, extra)

        @block.vector
        def _(dve):
            steps = [0]

            def link(ins):
                steps[0] += 1
                ins.then_inc(dve_step, 1)
                dve.wait_ge(dve_step, steps[0])

            dve.wait_ge(silu_c, 1)
            dve.tensor_copy(cbc[:], cact[:].unsqueeze(2).to_broadcast([P, C, P])).then_inc(cbc_ok, 1)
            dve.wait_ge(ld["pos"], 16)
            dve.wait_ge(consts, 5)
            link(dve.tensor_copy(posf[:], posi[:]))
            link(dve.tensor_tensor(ang[:], posf[:].unsqueeze(2).to_broadcast([P, T, RH]), freq[:].unsqueeze(1).to_broadcast([P, T, RH]), ALU.mult))
            link(dve.tensor_scalar(turns[:], ang[:], float(1.0 / (2 * np.pi)), MAGIC, ALU.mult, ALU.add))
            link(dve.tensor_scalar(turns[:], turns[:], -MAGIC, None, ALU.add))
            for piece in TWO_PI:
                link(dve.scalar_tensor_tensor(ang[:], turns[:], -piece, ang[:], ALU.mult, ALU.add))
            link(dve.tensor_scalar(ang[:], ang[:], PI_BELOW, -PI_BELOW, ALU.min, ALU.max))
            link(dve.scalar_tensor_tensor(turns[:], ang[:], -1.0, ang[:], ALU.mult, ALU.max))
            dve.tensor_scalar(turns[:], turns[:], -1.0, float(np.pi / 2), ALU.mult, ALU.add).then_inc(ang_ok, 1)
            dve.wait_ge(ld["x"], 16)
            for t in range(T):
                last = dve.tensor_tensor_reduce(h[:, t], x[:, t], x[:, t], 1.0, 0.0, ALU.mult, ALU.add, ss[:, t:t + 1])
            last.then_inc(ss_ok, 1)
            dve.wait_ge(std_ok, 1)
            link(dve.reciprocal(ss[:], ss[:]))
            dve.wait_ge(mod_ok, ADA_PE)
            dve.wait_ge(ld["gmix"], 16)
            dve.scalar_tensor_tensor(mod[:, G1], mod[:, G1], 1.0, gmix[:], ALU.add, ALU.mult).then_inc(g1_ok, 1)
            dve.wait_ge(g1_ok, 1)
            for t in range(T):
                link(dve.scalar_tensor_tensor(h[:, t], x[:, t], ss[:, t:t + 1], mod[:, G1], ALU.mult, ALU.mult))
                dve.tensor_tensor(h[:, t], h[:, t], mod[:, SH1], ALU.add).then_inc(h_ok, 1)
            dve.wait_ge(wsT_tr, 1)
            dve.tensor_copy(ws_raw[:], bank[2][:].rearrange("p (g n) -> p g n", g=GG)).then_inc(wsT_ok, 1)

            def ada_block(j):
                n = j - ADA_PE
                dve.wait_ge(ld_ada[j % 2], 16 * (j // 2 + 1))
                if n >= 2:
                    dve.wait_ge(ada_mm, j - 1)
                w = ada_w[j % 2]
                link(dve.tensor_scalar(acc[j % 2][:], w[:, 0, :], cact[:, 0:1], None, ALU.mult))
                for c in range(1, C):
                    ins = dve.scalar_tensor_tensor(acc[j % 2][:], w[:, c, :], cact[:, c:c + 1], acc[j % 2][:], ALU.mult, ALU.add)
                    if c < C - 1:
                        link(ins)
                ins.then_inc(acc_ok, 1)
                dve.wait_ge(acc_ok, n + 1)
                dve.engine_nop().then_inc(ada_dve, 1)

            dve.wait_ge(silu_c, 1)
            for t in range(T):
                ada_block(ADA_PE + 2 * t)
                ada_block(ADA_PE + 2 * t + 1)
                dve.wait_ge(proj_ok, NB * (t + 1))
                for g in range(GG):
                    last = dve.bn_stats(lnst[:, t * GG + g, :], v[:, t, g * P:(g + 1) * P])
                link(last)
                for g in range(GG):
                    dve.bn_aggr(lnmv[:, t * GG + g, :], lnst[:, t * GG + g, :])
                link(dve.tensor_tensor_reduce(lsq[:, 0:QL], lat[:, t, 0:QL], lat[:, t, 0:QL], 1.0, 0.0, ALU.mult, ALU.add, latss[:, t, 0:1]))
                last = dve.tensor_tensor_reduce(lsq[:, 0:KL], lat[:, t, QL:QL + KL], lat[:, t, QL:QL + KL], 1.0, 0.0, ALU.mult, ALU.add, latss[:, t, 1:2])
                if t < T - 1:
                    link(last)
            last.then_inc(stats_ok, 1)
            dve.wait_ge(lstd_ok, 3)
            link(dve.reciprocal(lnmv[:, :, 1], lnmv[:, :, 1]))
            dve.reciprocal(latss[:], latss[:]).then_inc(lrstd_ok, 1)
            dve.wait_ge(ld["small"], 16 * NSMALL)
            for t in range(T):
                for g in range(GG):
                    s = t * GG + g
                    last = dve.tensor_scalar(v[:, t, g * P:(g + 1) * P], v[:, t, g * P:(g + 1) * P], lnmv[:, s, 0:1], lnmv[:, s, 1:2], ALU.subtract, ALU.mult)
            link(last)
            link(dve.tensor_tensor(v[:], v[:], ln_g[:].unsqueeze(1).to_broadcast([P, T, GW]), ALU.mult))
            dve.tensor_tensor(v[:], v[:], ln_b[:].unsqueeze(1).to_broadcast([P, T, GW]), ALU.add).then_inc(v_ok, 1)
            for g in range(GG):
                dve.wait_ge(gate_mm, g + 1)
                dve.scalar_tensor_tensor(mixed[:, :, g * P:(g + 1) * P], bank[(7, 0, 1, 7)[g]][:].rearrange("p (t n) -> p t n", t=T), bsT[:, g:g + 1],
                                         u[:, :, g * P:(g + 1) * P], ALU.add, ALU.mult).then_inc(gate_ok, 1)
            link(dve.tensor_scalar(qn_g[:], qn_g[:], scale, None, ALU.mult))
            for i in range(2 * T):
                t, s = divmod(i, 2)
                dve.wait_ge(sq_ok, i + 1)
                dve.tensor_reduce(qkss[:, s, t, :], sq[:, s], AX.X, ALU.add).then_inc(ssq_ok, 1)
            dve.wait_ge(qstd_ok, 1)
            link(dve.reciprocal(qkss[:], qkss[:]))
            dve.wait_ge(trig_ok, 2)
            dve.wait_ge(ssq_ok, 2 * T)
            for s, (z, gain) in enumerate(((q, qn_g), (k, kn_g))):
                for t in range(T):
                    last = dve.tensor_tensor(z[:, t], z[:, t], qkss[:, s, t, :].unsqueeze(2).to_broadcast([P, H, QD]), ALU.mult)
                link(last)
                for t in range(T):
                    last = dve.tensor_tensor(z[:, t], z[:, t], gain[:].unsqueeze(1).to_broadcast([P, H, QD]), ALU.mult)
                link(last)
                z1, z2 = z[:, :, :, NOPE:NOPE + RH], z[:, :, :, NOPE + RH:QD]
                cb = cos[:].unsqueeze(2).to_broadcast([P, T, H, RH])
                sb_ = sin[:].unsqueeze(2).to_broadcast([P, T, H, RH])
                dve.tensor_tensor(rt[0][:], z1, cb, ALU.mult)
                dve.tensor_tensor(rt[1][:], z2, sb_, ALU.mult)
                dve.tensor_tensor(rt[2][:], z1, sb_, ALU.mult)
                link(dve.tensor_tensor(rt[3][:], z2, cb, ALU.mult))
                dve.tensor_tensor(z1, rt[0][:], rt[1][:], ALU.subtract)
                dve.tensor_tensor(z2, rt[2][:], rt[3][:], ALU.add).then_inc(qk_ok, 1)
                dve.wait_ge(qk_ok, s + 1)

            def row_max(i):
                t, hd = divmod(i, H)
                dve.wait_ge(s_mm, i + 1)
                link(dve.memset(bank[i % 3][0:CHUNK, t * P + CHUNK:(t + 1) * P], NEG))
                dve.tensor_reduce(nmax[:, t, hd:hd + 1], bank[i % 3][:, 0:(t + 1) * P], AX.X, ALU.max, negate=True).then_inc(nmax_ok, 1)

            def outputs(t):
                dve.wait_ge(av_mm, (t + 1) * H)
                link(dve.reciprocal(den[:, t, :], den[:, t, :]))
                dve.tensor_tensor(mixed[:, t, GW:D].rearrange("p (h d) -> p h d", h=H), bank[6 + t % 2][:].rearrange("p (h d) -> p h d", h=H),
                                  den[:, t, :].unsqueeze(2).to_broadcast([P, H, VD]), ALU.mult).then_inc(o_ok, 1)
                dve.wait_ge(o_ok, t + 1)
                for s in range(2):
                    last = dve.tensor_tensor_reduce(osq[:, s * GW:(s + 1) * GW], mixed[:, t, s * GW:(s + 1) * GW], mixed[:, t, s * GW:(s + 1) * GW], 1.0, 0.0, ALU.mult, ALU.add, oss[:, t, s:s + 1])
                if t < T - 1:
                    link(last)
                else:
                    last.then_inc(oss_ok, 1)

            dve.wait_ge(gate_ok, GG)
            for i in range(NI):
                row_max(i)
                if i % H == 3 and i > H:
                    outputs(i // H - 1)
            outputs(T - 1)
            dve.wait_ge(ostd_ok, 1)
            dve.reciprocal(oss[:], oss[:]).then_inc(orstd_ok, 1)
            dve.wait_ge(ld["gffn"], 16)
            dve.wait_ge(mod_ok, ADA)
            dve.scalar_tensor_tensor(mod[:, G2], mod[:, G2], 1.0, gffn[:], ALU.add, ALU.mult).then_inc(g2_ok, 1)
            dve.wait_ge(g2_ok, 1)

            def residual(t):
                for m in range(2):
                    i = 2 * t + m
                    cols = slice(m * BANK, (m + 1) * BANK)
                    dve.wait_ge(out_mm, i + 1)
                    dve.tensor_tensor(xtmp[:, cols], bank[i % 4][:], mod[:, GATE1, cols], ALU.mult).then_inc(x1_ok, 1)
                    dve.wait_ge(x1_ok, i + 1)
                    link(dve.tensor_tensor(x[:, t, cols], x[:, t, cols], xtmp[:, cols], ALU.add))
                dve.tensor_tensor_reduce(h2[:, t], x[:, t], x[:, t], 1.0, 0.0, ALU.mult, ALU.add, ss[:, t:t + 1]).then_inc(ss2_ok, 1)

            def norm2(t):
                dve.wait_ge(std2_ok, t + 1)
                link(dve.reciprocal(ss[:, t:t + 1], ss[:, t:t + 1]))
                link(dve.scalar_tensor_tensor(h2[:, t], x[:, t], ss[:, t:t + 1], mod[:, G2], ALU.mult, ALU.mult))
                dve.tensor_tensor(h2[:, t], h2[:, t], mod[:, SH2], ALU.add).then_inc(h2_ok, 1)

            residual(0)
            for t in range(T):
                if t + 1 < T:
                    residual(t + 1)
                norm2(t)
            dve.wait_ge(sco_ok, 1)
            link(dve.tensor_tensor(bia[:], sco[:], rbias[:].unsqueeze(1).to_broadcast([P, T, NE]), ALU.add))
            for i in range(T * N_GROUPS):
                t, g = divmod(i, N_GROUPS)
                last = dve.max(m8[:, i, :], bia[:, t, g * EG:(g + 1) * EG])
            link(last)
            link(dve.tensor_tensor(gsum[:].rearrange("p t g -> p (t g)"), m8[:, :, 0], m8[:, :, 1], ALU.add))
            other = gsum[:].unsqueeze(2).to_broadcast([P, T, N_GROUPS, N_GROUPS])
            own = gsum[:].unsqueeze(3).to_broadcast([P, T, N_GROUPS, N_GROUPS])
            dve.tensor_tensor(cgt[:], other, own, ALU.is_gt)
            link(dve.tensor_tensor(cge[:], other, own, ALU.is_ge))
            link(dve.tensor_tensor(cge[:], cge[:], gtri[:].unsqueeze(1).to_broadcast([P, T, N_GROUPS, N_GROUPS]), ALU.mult))
            link(dve.tensor_tensor(cge[:], cge[:], cgt[:], ALU.max))
            link(dve.tensor_reduce(grank[:], cge[:], AX.X, ALU.add))
            link(dve.tensor_scalar(gmask[:], grank[:], float(TOPK_GROUPS) - 0.5, None, ALU.is_lt))
            link(dve.tensor_scalar(gneg[:], gmask[:], 1.0, -NEG, ALU.subtract, ALU.mult))
            ge = lambda z: z[:].rearrange("p t (g e) -> p t g e", g=N_GROUPS)
            eb = lambda z: z[:].unsqueeze(3).to_broadcast([P, T, N_GROUPS, EG])
            link(dve.tensor_tensor(ge(bia), ge(bia), eb(gmask), ALU.mult))
            link(dve.tensor_tensor(ge(bia), ge(bia), eb(gneg), ALU.add))
            for t in range(T):
                last = dve.max(v8[:, t, :], bia[:, t, :])
            link(last)
            for t in range(T):
                last = dve.match_replace(rep[:, t, :], v8[:, t, :], bia[:, t, :], 4.0 * NEG)
            link(last)
            dve.wait_ge(st_h2, 16 * T)
            dve.wait_ge(h2T_tr, 2 * T)
            dve.tensor_tensor(selm[:], rep[:], bia[:], ALU.not_equal).then_inc(selm_ok, 1)
            dve.wait_ge(selm_ok, 1)
            link(dve.tensor_tensor(comb[:], selm[:], sco[:], ALU.mult))
            link(dve.tensor_reduce(wsum[:], comb[:], AX.X, ALU.add))
            link(dve.reciprocal(wsum[:], wsum[:]))
            link(dve.scalar_tensor_tensor(pay[:, :, :, 2], comb[:], ROUTED_SCALE, wsum[:].unsqueeze(2).to_broadcast([P, T, NE]), ALU.mult, ALU.mult))
            link(dve.memset(zero[:], 0.0))
            for t in range(T):
                last = dve.tensor_tensor_scan(rank[:, t, :], selm[:, t, :], zero[:, 0:NE], 0.0, ALU.add, ALU.add)
            link(last)
            dve.tensor_scalar(pay[:, :, :, 0], tok[:].unsqueeze(2).to_broadcast([P, T, NE]), -BIG, None, ALU.add)
            dve.memset(pay[:, :, :, 3], 0.0)
            link(dve.tensor_scalar(posx[:], tok[:], float(TOP_K), -BIG - 1.0, ALU.mult, ALU.add))
            link(dve.tensor_tensor(pay[:, :, :, 1], rank[:], posx[:].unsqueeze(2).to_broadcast([P, T, NE]), ALU.add))

            def shared_hidden(t):
                dve.wait_ge(ssilu_ok, t + 1)
                if t >= 2:
                    dve.wait_ge(shT_tr, t - 1)
                dve.tensor_tensor(hw[t % 2][:], bank[t % 2][:, FF:2 * FF], sgate[t % 2][:], ALU.mult).then_inc(shw_ok, 1)

            def shared_out(t):
                dve.wait_ge(sd_mm, t + 1)
                for m in range(2):
                    last = dve.tensor_tensor(xtmp[:, m * BANK:(m + 1) * BANK], bank[2 + m][:], mod[:, GATE2, m * BANK:(m + 1) * BANK], ALU.mult)
                link(last)
                dve.tensor_tensor(x[:, t], x[:, t], xtmp[:], ALU.add).then_inc(sh_ok, 1)
                dve.wait_ge(sh_ok, t + 1)

            shared_hidden(0)
            dve.wait_ge(pos_mm, 1)
            pos = bank[6][:, 0:T * NE].rearrange("p (t e) -> p t e", t=T)
            dve.tensor_copy(cnt[:], bank[6][:, T * NE:(T + 1) * NE])
            link(dve.scalar_tensor_tensor(posm[:], pos, 1.0, selm[:], ALU.add, ALU.mult))
            dve.tensor_scalar(posm[:], posm[:], -1.0, None, ALU.add).then_inc(pay_ok, 1)
            dve.wait_ge(pay_ok, 1)

            iota_b = iota[:].unsqueeze(1).to_broadcast([P, T, P])

            def one_hot(i, slots, n):
                wait(dve, idx_mm, n + (-1))
                dve.tensor_tensor(onehot[i][:], slots.to_broadcast([P, T, P]), iota_b, ALU.is_equal).then_inc(oh_ok, 1)

            def index_rows(j, n):
                dve.wait_ge(idx_mm, n + 1)
                dve.tensor_scalar(src_i[j][:], bank[6][:, 0:2], BIG, None, ALU.add)
                dve.tensor_copy(combw[j][:], bank[6][:, 2:3]).then_inc(idx_ok, 1)

            def hidden(j, i, n):
                dve.wait_ge(silu_ok, n + 1)
                wait(dve, hwT_tr, n + (-1))
                dve.scalar_tensor_tensor(hw[i][:], bank[2 + i][:, FF:2 * FF], combw[j][:], sgate[i][:], ALU.mult, ALU.mult).then_inc(hw_ok, 1)

            def rows_copy(i, n):
                dve.wait_ge(xeT_tr, n + 1)
                dve.tensor_copy(xeT[i][:, 4:8, :], bank[1][:].rearrange("p (c n) -> p c n", c=4)).then_inc(xeT_v, 1)

            def out_copy(i, n, stores):
                dve.wait_ge(d_mm, n + 1)
                wait(dve, st_y[i], stores)
                dve.tensor_copy(oute[i][:, BANK:D], bank[5][:]).then_inc(oute_v, 1)

            def one_hot_of(E):
                one_hot(E[1] % 2, posm[:, :, bass.ds(num(E), 1)], num(E))

            def rows_copy_of(E):
                if not (E[0] is None and E[1] < 2):
                    dve.wait_ge(gu_mm, num(E, -1))
                rows_copy(E[1] % 2, num(E))

            one_hot_of((None, 0))
            one_hot_of((None, 1))
            index_rows(0, 0)
            one_hot_of((None, 2))
            index_rows(1, 1)
            dve.wait_ge(pool_step, 1)
            for b in range(3):
                last = dve.tensor_scalar(flag[:, b * NE:(b + 1) * NE], cnt[:], float((b + 1) * P) + 0.5, None, ALU.is_gt)
            link(last)
            link(dve.tensor_tensor_scan(runs[:], flag[:], zero[:], 0.0, ALU.add, ALU.add))
            dve.tensor_copy(nextra[:], runs[:, 3 * NE - 1:3 * NE]).then_inc(list_ok, 1)
            dve.wait_ge(list_ok, 1)
            link(dve.tensor_scalar(runs[:], runs[:], part[:], 1.0, ALU.subtract, ALU.is_equal))
            link(dve.tensor_tensor(flag[:], flag[:], runs[:], ALU.mult))
            for s in range(2):
                link(dve.tensor_tensor_reduce(ltmp[:], flag[:], eblk[:, s].rearrange("p b e -> p (b e)"), 1.0, 0.0, ALU.mult, ALU.add, lcol[:, s:s + 1]))
            for s in range(2):
                last = dve.tensor_scalar(lmat[0:MAXX, s, :], ident[0:MAXX, 0:MAXX], lcol[0:MAXX, s:s + 1], None, ALU.mult)
            last.then_inc(lmat_ok, 1)
            index_rows(2, 2)
            one_hot_of((None, 3))
            dve.wait_ge(list_mm, 1)
            dve.tensor_copy(list_i[:], bank[6][:, 0:2 * MAXX])
            dve.tensor_copy(list_f[:], bank[6][:, 0:2 * MAXX]).then_inc(list_ok, 1)
            shared_hidden(1)
            for t in range(T):
                shared_out(t)
                if t + 2 < T:
                    shared_hidden(t + 2)
            rows_copy_of((None, 0))
            hidden(0, 0, 0)
            rows_copy_of((None, 1))

            def step(E):
                E1, E2, E3, E4 = (after(E, d) for d in (1, 2, 3, 4))
                if exists(E1):
                    hidden(E1[1] % 4, E1[1] % 2, num(E1))
                if exists(E3):
                    if not (E[0] is None and E[1] < 1):
                        dve.wait_ge(st_y[(E[1] + 1) % 2], times16(pairs(after(E, -1))))
                    index_rows(E3[1] % 4, num(E3))
                if exists(E4):
                    one_hot_of(E4)
                if exists(E2):
                    rows_copy_of(E2)
                out_copy(E[1] % 2, num(E), times16(pairs(E, -1)))

            every_expert(dve, step)

            def extra(i):
                e = dve.value_load(list_i[0:1, bass.ds(i, 1)], min_val=0, max_val=NE - 1)
                n = i + NE
                dve.wait_ge(st_y[0], i * 16 + 16 * EXTRA0)
                dve.wait_ge(idx_mm, n)
                dve.tensor_scalar(posx[:], posm[:, :, bass.ds(e, 1)].rearrange("p t o -> p (t o)"), list_f[:, bass.ds(i + MAXX, 1)], None, ALU.subtract).then_inc(posx_ok, 1)
                dve.wait_ge(posx_ok, i + 1)
                one_hot(0, posx[:].unsqueeze(2), n)
                index_rows(0, n)
                rows_copy(0, n)
                hidden(0, 0, n)
                out_copy(0, n, i * 16 + 16 * EXTRA0)

            extra_blocks(dve, extra)
            for t in range(T):
                y = yrows[t % 2]
                dve.wait_ge(ld_y[t % 2], 16 * (t // 2 + 1))
                link(dve.tensor_tensor(y[:, 0:4], y[:, 0:4], y[:, 4:8], ALU.add))
                link(dve.tensor_tensor(y[:, 0:2], y[:, 0:2], y[:, 2:4], ALU.add))
                link(dve.tensor_tensor(y[:, 0], y[:, 0], y[:, 1], ALU.add))
                link(dve.tensor_tensor(y[:, 0], y[:, 0], mod[:, GATE2], ALU.mult))
                dve.tensor_tensor(x[:, t], x[:, t], y[:, 0], ALU.add).then_inc(fin_ok, 1)


def times16(n, by=16):
    return n * by


def kernel(**inputs):
    import concourse.bacc as bacc
    from concourse.bass_utils import run_bass_kernel_spmd

    nc = bacc.Bacc("TRN2", target_bir_lowering=False, num_devices=1)
    arrays = {f"in_{name}": np.ascontiguousarray(v) for name, v in inputs.items()}
    aps = {name: nc.dram_tensor(f"in_{name}", inputs[name].shape, mybir.dt.from_np(arrays[f"in_{name}"].dtype), kind="ExternalInput").ap() for name in inputs}
    out = nc.dram_tensor("out", inputs["x"].shape, F32, kind="ExternalOutput").ap()
    trunk_kernel(nc, aps, out)
    r = run_bass_kernel_spmd(nc, [arrays], core_ids=[0])
    return r.results[0]["out"]
```

```python
from contextlib import ExitStack

import numpy as np

import concourse.bass as bass
from concourse import mybir

F32 = mybir.dt.float32
F32R = mybir.dt.float32r
I32 = mybir.dt.int32
ALU = mybir.AluOpType
ACT = mybir.ActivationFunctionType
AX = mybir.AxisListType

P = 128
KB = 1024
BIG = 8192.0
NEG = -1.0e30
EPS = 1e-6
CHUNK = 64
TOP_K = 8
N_GROUPS = 8
TOPK_GROUPS = 4
ROUTED_SCALE = 2.5
ROPE_THETA = 10000.0
TWO_PI = (6.28125, 0.00193500518798828125, float(2 * np.pi - 6.28125 - 0.00193500518798828125))
PI_BELOW = 3.1415925
MAGIC = 1.5 * 2.0 ** 23


def trunk_kernel(nc, a, out):
    S, D = a["x"].shape[1:]
    T = S // P
    C = D // P
    GW = a["gm_ln_g"].shape[1] * a["gm_ln_g"].shape[2]
    GG, GB = a["gm_ws"].shape[1:3]
    QL, KL = a["q_a_g"].shape[1], a["kv_a_g"].shape[1]
    QC, KC = QL // P, KL // P
    QD = a["q_norm_g"].shape[1]
    H = a["w_q_up"].shape[2] // QD
    KVD = a["w_kv_up"].shape[2] // H
    VD = (D - GW) // H
    NOPE = KVD - VD
    ROPE = QD - NOPE
    RH = ROPE // 2
    IN = a["w_in"].shape[2]
    LAT = IN - 2 * GW
    NE, _, FF = a["w_exp_gate"].shape[1:]
    FC = FF // P
    EG = NE // N_GROUPS
    BANK = 512
    ADA = a["w_ada"].shape[2] // BANK
    ADA_PE = (0, 2)
    ADA_DVE = tuple(j for j in range(ADA) if j not in ADA_PE)
    ADA_FIRST = 4
    MAXX = 32
    NSMALL = 9
    scale = float(QD) ** -0.5
    inv_freq = (1.0 / (np.float32(ROPE_THETA) ** (np.arange(0, ROPE, 2, dtype=np.float32) / np.float32(ROPE)))).astype(np.float32)

    h2_dram = nc.dram_tensor("h2_rows", [S, D], F32).ap()
    y_dram = nc.dram_tensor("expert_sums", [S + P, D], F32).ap()

    with ExitStack() as ctx:
        SLAB = 207 * KB
        ctx.enter_context(nc.sbuf_tensor("slab", [P, SLAB // 4], F32))
        base = nc.sbuf_base - SLAB

        def at(name, kb, shape, dt=F32):
            return nc.alloc_sbuf_tensor_at(name, shape, dt, offset=base + int(kb * KB))

        def sem(name):
            return ctx.enter_context(nc.semaphore(name))

        bank = [ctx.enter_context(nc.psum_tensor(f"bank{i}", [P, BANK], F32)) for i in range(8)]

        x = at("x_sb", 0, [P, T, D])
        mod = at("mod_rows", 16, [P, 6, D])
        SH1, G1, GATE1, SH2, G2, GATE2 = range(6)
        w_u = at("w_u_sb", 40, [P, C, GW])
        w_v = at("w_v_sb", 56, [P, C, GW])
        w_lat = at("w_lat_sb", 72, [P, C, LAT])
        ada_w = [at(f"ada_w{i}", kb, [P, C, BANK]) for i, kb in enumerate((94, 110, 167, 40))]
        h = at("h_sb", 126, [P, T, D])
        hT = at("hT", 143, [P, C, S])
        cbc = at("cbc", 159, [P, C, P])
        gmix = at("gmix", 163, [P, D])
        bias0 = [at(f"bias0_{i}", 163 + 2 * i, [P, BANK]) for i in range(2)]
        u = at("u_sb", 159, [P, T, GW])
        v = at("v_sb", 167, [P, T, GW])
        lat = at("lat_sb", 175, [P, T, LAT])
        w_q = at("w_q_sb", 126, [P, QC, H * QD])
        w_kv = at("w_kv_sb", 135, [P, KC, H * KVD])
        q = at("q_sb", 96, [P, T, H, QD])
        k = at("k_sb", 108, [P, T, H, QD])
        sq = at("sq_sb", 120, [P, 2, H, QD])
        rt = [at(f"rope_t{i}", 120 + 2 * i, [P, T, H, RH]) for i in range(4)]
        vv = at("vv_sb", 72, [P, T, H, VD])
        qT = at("qT", 80, [P, H, S])
        kT = at("kT", 159, [P, H, S])
        w_q_high = at("w_q_high", 80, [P, QC, H * QD], F32R)
        w_q_low = at("w_q_low", 126, [P, QC, H * QD], F32R)
        w_kv_high = [at(f"w_kv_high{i}", kb, [P, H * KVD], F32R) for i, kb in enumerate((159, 89))]
        w_kv_low = at("w_kv_low", 135, [P, KC, H * KVD], F32R)
        latT_high = at("latT_high", 56, [P, QC + KC, S], F32R)
        latT_low = [at(f"latT_low{i}", kb, [P, S], F32R) for i, kb in enumerate((66, 68, 70, 163, 165))]
        assert (QC, KC) == (3, 2)
        NPB = 3
        NSB, NTB = 4, 2
        prob = [at(f"prob{i}", 112 + 2 * i, [P, S]) for i in range(NPB)]
        probT = [at(f"probT{i}", 118 + 2 * i, [P, S]) for i in range(NPB)]
        mixed = at("mixed", 143, [P, T, D])
        osq = at("osq", 130, [P, D])
        w_out = at("w_out_sb", 40, [P, C, D])
        w_out_high = [at(f"w_out_high{i}", kb, [P, C // 4, D], F32R) for i, kb in enumerate((96, 104, 175, 134))]
        w_out_low = at("w_out_low", 40, [P, C, D], F32R)
        mixT_high = at("mixT_high", 80, [P, C, S], F32R)
        mixT_low = at("mixT_low", 159, [P, C, S], F32R)
        h2 = at("h2_sb", 143, [P, T, D])
        h2T = at("h2T", 112, [P, C, S])
        w_r = at("w_r_sb", 128, [P, C, NE])
        xtmp = at("xtmp", 130, [P, D])
        gffn = at("gffn", 124, [P, D])
        ws_g = at("ws_g", 159, [P, C, FF])
        ws_u = at("ws_u", 167, [P, C, FF])
        ws_d = at("ws_d", 175, [P, FC, D])
        sco = at("sco", 151, [P, T, NE])
        bia = at("bia", 152, [P, T, NE])
        rep = at("rep", 153, [P, T, NE])
        m8 = at("m8", 154, [P, T * N_GROUPS, 8])
        cge = at("cge", 155, [P, T, N_GROUPS, N_GROUPS])
        cgt = at("cgt", 156, [P, T, N_GROUPS, N_GROUPS])
        comb = at("comb", 158, [P, T, NE])
        gsum = at("gsum", 130, [P, T, N_GROUPS])
        gmask = at("gmask", 130.25, [P, T, N_GROUPS])
        gneg = at("gneg", 130.5, [P, T, N_GROUPS])
        grank = at("grank", 130.75, [P, T, N_GROUPS])
        v8 = at("v8", 131, [P, T, 8])
        wsum = at("wsum", 131.25, [P, T])
        zero = at("zero", 131.5, [P, 3 * NE])
        flag = at("flag", 132.25, [P, 3 * NE])
        runs = at("runs", 133, [P, 3 * NE])
        lcol = at("lcol", 151, [P, 2])
        lmat = at("lmat", 151.5, [P, 2, MAXX])
        ltmp = at("ltmp", 152, [P, 3 * NE])
        eblk = at("eblk", 153, [P, 2, 3, NE])
        HC = C // 2
        w_gu = [[at(f"w_gu{half}_{i}", 40 + 16 * half + 8 * i, [P, 2, HC, FF]) for i in range(2)] for half in range(2)]
        w_d = [at(f"w_d{i}", 72 + 8 * i, [P, FC, D]) for i in range(2)]
        gu_high = [at(f"gu_high{half}", kb, [P, 2, HC, FF], F32R) for half, kb in enumerate((16, 88))]
        gu_low = [at(f"gu_low{half}", kb, [P, 2, HC, FF], F32R) for half, kb in enumerate((24, 102))]
        d_high = at("d_high", 112, [P, FC, D], F32R)
        d_low = at("d_low", 120, [P, FC, D], F32R)
        oute = [at(f"oute{i}", 159 + 4 * i, [P, D]) for i in range(2)]
        pay = at("pay", 96, [P, T, NE, 2])
        selm = at("selm", 100, [P, T, NE])
        posm = at("posm", 101, [P, T, NE])
        onehot = [at(f"onehot{i}", 134 + 2 * i, [P, T, P]) for i in range(2)]
        sgate = [at(f"sgate{i}", 138 + i, [P, FF]) for i in range(2)]
        hw = [at(f"hw{i}", 140 + i, [P, FF]) for i in range(2)]
        hwT = at("hwT", 142, [P, FC, P])
        hwT_high = at("hwT_high", 183, [P, FC, P], F32R)
        hwT_low = at("hwT_low", 184, [P, FC, P], F32R)
        xe = [at(f"xe{i}", 143 + 4 * i, [P, D]) for i in range(2)]
        xeT_high = [at("xeT_high0", 151, [P, C, P], F32R)]
        xeT_low = [at("xeT_low0", 155, [P, C, P], F32R)]
        place = [186.0]

        def small(name, shape, dt=F32):
            t = at(name, place[0], shape, dt)
            place[0] += -(-int(np.prod(shape[1:])) // 8) / 32
            assert place[0] <= 207, name
            return t

        ident = small("ident", [P, P])
        ones = small("ones", [P, P])
        tri = small("tri", [P, P])
        gtri = small("gtri", [P, N_GROUPS, N_GROUPS])
        iota = small("iota", [P, P])
        tok = small("tok", [P, T])
        part = small("part", [P, 1])
        spare = small("spare", [P, 1])
        epsc = small("epsc", [P, 1])
        freq = small("freq", [P, RH])
        cT = small("cT", [P, C])
        cact = small("cact", [P, C])
        b_ada = small("b_ada_rows", [P, BANK])
        zeros = at("zeros", place[0], [P, D])
        acc = [small(f"ada_acc{i}", [P, BANK]) for i in range(2)]
        ss = small("ss", [P, T])
        lnst = small("lnst", [P, T * GG, 6])
        lnmv = small("lnmv", [P, T * GG, 2])
        latss = small("latss", [P, T, 2])
        qkss = small("qkss", [P, 2, T, H])
        oss = small("oss", [P, T, 2])
        xeT_high.append(at("xeT_high1", place[0], [P, C, P], F32R))
        xeT_low.append(at("xeT_low1", place[0] + 4, [P, C, P], F32R))
        ln_g = small("ln_g", [P, GW])
        ln_b = small("ln_b", [P, GW])
        ws_raw = small("ws_raw", [P, GG, GB])
        lsq = at("lsq", place[0], [P, QL])
        ws_low = small("ws_low", [P, GG, GB])
        bsT = small("bsT", [P, GG])
        qa_g = small("qa_g", [P, QC])
        kva_g = small("kva_g", [P, KC])
        qn_g = small("qn_g", [P, QD])
        kn_g = small("kn_g", [P, QD])
        on_g = small("on_g", [P, C])
        rbias = small("rbias", [P, NE])
        posi = small("posi", [P, T], I32)
        posf = small("posf", [P, T])
        ang = small("ang", [P, T, RH])
        turns = small("turns", [P, T, RH])
        cos = small("cos", [P, T, RH])
        sin = small("sin", [P, T, RH])
        den = small("den", [P, T, H])
        nmax = small("nmax", [P, T, H])
        src_i = [small(f"src_i{i}", [P, 1], I32) for i in range(4)]
        slots = [small(f"slots{i}", [P, 2]) for i in range(4)]
        dst_i = [small(f"dst_i{i}", [P, 1], I32) for i in range(2)]
        list_i = small("list_i", [P, 2 * MAXX], I32)
        list_f = small("list_f", [P, 2 * MAXX])
        nextra = small("nextra", [P, 1], I32)
        cnt = small("cnt", [P, NE])
        posx = small("posx", [P, T])

        ld = {n: sem("ld_" + n) for n in ("x", "c", "bada", "pos", "gmix", "gffn", "small", "ws", "wlat", "wv", "wu", "wq", "wr", "wsh", "wsd")}
        ld_ada = [sem(f"ld_ada{i}") for i in range(4)]
        ld_wout = [sem("ld_wout0"), sem("ld_wout1")]
        ld_bias = [sem("ld_bias0"), sem("ld_bias1")]
        (consts, dve_step, pool_step, silu_c, cbc_ok, ada_pe, ada_dve, acc_ok, ada_mm, mod_ok, g1_ok,
         g2_ok, ss_ok, std_ok, h_ok, hT_tr, hT_ok, wsT_tr, wsT_ok, proj_mm, proj_ok) = (sem(n) for n in (
            "consts", "dve_step", "pool_step", "silu_c", "cbc_ok", "ada_pe", "ada_dve", "acc_ok", "ada_mm",
            "mod_ok", "g1_ok", "g2_ok", "ss_ok", "std_ok", "h_ok", "hT_tr", "hT_ok", "wsT_tr", "wsT_ok", "proj_mm", "proj_ok"))
        (stats_ok, vstats_ok, vstd_ok, lstd_ok, lrstd_ok, latn_ok, latT_tr, latT_ok, v_ok, gate_mm, gate_ok, kpe_ok, up_mm, up_ok, sq_ok,
         ssq_ok, qstd_ok, ang_ok, trig_ok, qk_ok, qkT_tr, qkT_ok) = (sem(n) for n in (
            "stats_ok", "vstats_ok", "vstd_ok", "lstd_ok", "lrstd_ok", "latn_ok", "latT_tr", "latT_ok", "v_ok", "gate_mm", "gate_ok", "kpe_ok",
            "up_mm", "up_ok", "sq_ok", "ssq_ok", "qstd_ok", "ang_ok", "trig_ok", "qk_ok", "qkT_tr", "qkT_ok"))
        (s_mm, nmax_ok, exp_ok, pT_tr, pT_ok, av_mm, o_ok, mix_v, oss_ok, ostd_ok, orstd_ok, mix_ok, mixT_tr, out_mm,
         x1_ok, ss2_ok, std2_ok, h2_ok, st_h2, h2T_tr, h2T_ok, rt_mm, sco_ok, selm_ok, pos_mm, pay_ok, lmat_ok, list_mm,
         list_ok) = (sem(n) for n in (
            "s_mm", "nmax_ok", "exp_ok", "pT_tr", "pT_ok", "av_mm", "o_ok", "mix_v", "oss_ok", "ostd_ok", "orstd_ok", "mix_ok",
            "mixT_tr", "out_mm", "x1_ok", "ss2_ok", "std2_ok", "h2_ok", "st_h2", "h2T_tr", "h2T_ok", "rt_mm",
            "sco_ok", "selm_ok", "pos_mm", "pay_ok", "lmat_ok", "list_mm", "list_ok"))
        (sgu_mm, ssilu_ok, shw_ok, shT_tr, shT_ok, sd_mm, sh_ok) = (sem(n) for n in (
            "sgu_mm", "ssilu_ok", "shw_ok", "shT_tr", "shT_ok", "sd_mm", "sh_ok"))
        ld_gu = [[sem(f"ld_gu{half}_{i}") for i in range(2)] for half in range(2)]
        ld_d = [sem("ld_d0"), sem("ld_d1")]
        ld_xe = [sem("ld_xe0"), sem("ld_xe1")]
        gu_high_ok = [sem("gu_high0_ok"), sem("gu_high1_ok")]
        gu_low_ok = [sem("gu_low0_ok"), sem("gu_low1_ok")]
        (d_high_ok, d_low_ok, xe_high_ok, xe_low_ok, hwT_high_ok, hwT_low_ok, gu_mm0, st_y, st_zero, bias_zero, wup_high_ok, wup_ok, latT_low_ok, wout_high_ok, wout_ok, mixT_high_ok, mixT_low_ok) = (sem(n) for n in (
            "d_high_ok", "d_low_ok", "xe_high_ok", "xe_low_ok", "hwT_high_ok", "hwT_low_ok", "gu_mm0", "st_y", "st_zero", "bias_zero", "wup_high_ok", "wup_ok", "latT_low_ok", "wout_high_ok", "wout_ok", "mixT_high_ok", "mixT_low_ok"))
        (oh_ok, idx_mm, idx_ok, zeros_set, xeT_tr, gu_mm, silu_ok, hw_ok, hwT_tr, d_mm,
         oute_ok, st_x, st_out, posx_ok) = (sem(n) for n in (
            "oh_ok", "idx_mm", "idx_ok", "zeros_set", "xeT_tr", "gu_mm", "silu_ok", "hw_ok", "hwT_tr", "d_mm",
            "oute_ok", "st_x", "st_out", "posx_ok"))

        def num(E, d=0):
            m, r = E
            return r + d if m is None else m * 4 + (r + d)

        def pairs(E, d=0):
            m, r = E
            return r // 2 + 1 + d if m is None else m * 2 + (r // 2 + 1 + d)

        def after(E, d):
            return E[0], E[1] + d

        def exists(E):
            return E[0] is not None or E[1] < NE

        def first(E):
            return E[0] is None and E[1] == 0

        def wait(eng, s, value):
            if not isinstance(value, int) or value > 0:
                eng.wait_ge(s, value)

        apart_sem = {"sp": sem("sp_apart"), "pool": sem("pool_apart")}

        def apart(eng, name):
            eng.sem_inc(apart_sem[name], 1)

        HEAD = 4

        def every_expert(eng, step):
            for r in range(HEAD):
                step((None, r))
            with eng.Fori(0, (NE - 2 * HEAD) // 4) as m:
                for r in range(4):
                    step((m, HEAD + r))
            for r in range(NE - HEAD, NE):
                step((None, r))

        def extra_blocks(eng, step):
            eng.wait_ge(list_ok, 2)
            n = eng.value_load(nextra[0:1, 0:1], min_val=0, max_val=MAXX)
            with eng.If(n > 0):
                with eng.Fori(0, n) as i:
                    step(i)
            return n

        def ada_buffer(j):
            return (j, 16) if j < ADA_FIRST else (j % 2, 16 * (j // 2))

        def shared_banks(t):
            return ((3, 2), (0, 1), (0, 1), (4, 5))[t]

        x_dram = a["x"].rearrange("b (t p) d -> p (b t) d", p=P)
        w_ada_v = a["w_ada"][0].rearrange("(p c) n -> p c n", c=C)

        def bcast(ap, n):
            return ap.rearrange("l n -> (l n)").unsqueeze(0).to_broadcast([P, n])

        lat_cuts = [(n0, min(n0 + BANK, LAT)) for n0 in range(0, LAT, BANK)]
        NL = len(lat_cuts)
        V0 = T * NL
        U0 = V0 + T
        NI = T * H
        EXTRA0 = NE // 2

        block = ctx.enter_context(nc.Block())

        @block.sync
        def _(sp):
            sp.dma_start(cT[:], a["c"].rearrange("b (p c) -> p (b c)", c=C)).then_inc(ld["c"], 16)
            w_in_v = a["w_in"][0].rearrange("(p c) n -> p c n", c=C)
            for j in range(ADA):
                i, _ = ada_buffer(j)
                if j >= ADA_FIRST:
                    before = j - ADA_FIRST if j < ADA_FIRST + 2 else j - 2
                    if before in ADA_PE:
                        sp.wait_ge(ada_pe, ADA_PE.index(before) + 1)
                    else:
                        sp.wait_ge(ada_dve, ADA_DVE.index(before) + 1)
                sp.dma_start(ada_w[i][:], w_ada_v[:, :, j * BANK:(j + 1) * BANK]).then_inc(ld_ada[i], 16)
                if j == 1:
                    sp.dma_start(x[:], x_dram).then_inc(ld["x"], 16)
                if j == ADA_FIRST - 1:
                    sp.dma_start(w_lat[:], w_in_v[:, :, 2 * GW:]).then_inc(ld["wlat"], 16)
                if j == ADA_FIRST + 1:
                    sp.wait_ge(bias_zero, 1)
                for b in {ADA_FIRST + 1: (ADA_FIRST, ADA_FIRST + 1)}.get(j, (j,) if j > ADA_FIRST + 1 else ()):
                    sp.dma_start(bias0[b % 2][0:1, :], a["b_ada"][:, b * BANK:(b + 1) * BANK]).then_inc(ld_bias[b % 2], 16)
                if j == ADA_FIRST + 1:
                    sp.dma_start(w_v[:], w_in_v[:, :, GW:2 * GW]).then_inc(ld["wv"], 16)
                    sp.wait_ge(ada_dve, 2)
                    sp.dma_start(w_u[:], w_in_v[:, :, 0:GW]).then_inc(ld["wu"], 16)
                if j == ADA_FIRST + 4:
                    sp.wait_ge(hT_tr, 2 * T)
                    sp.dma_start(w_q[:], a["w_q_up"][0].rearrange("(p c) n -> p c n", c=QC)).then_inc(ld["wq"], 16)
                    sp.dma_start(w_kv[:], a["w_kv_up"][0].rearrange("(p c) n -> p c n", c=KC)).then_inc(ld["wq"], 16)
            w_out_v = a["w_out"][0].rearrange("(p c) n -> p c n", c=C)
            sp.wait_ge(up_mm, 4 * T)
            sp.dma_start(w_out[:, C // 2:C], w_out_v[:, C // 2:C]).then_inc(ld_wout[1], 16)
            sp.wait_ge(proj_mm, U0 + T)
            sp.dma_start(w_out[:, 0:C // 2], w_out_v[:, 0:C // 2]).then_inc(ld_wout[0], 16)
            sp.dma_start(w_r[:], a["w_router"][0].rearrange("(p c) n -> p c n", c=C)).then_inc(ld["wr"], 16)
            sp.wait_ge(qk_ok, 2)
            sp.dma_start(gffn[:], bcast(a["norm_ffn_g"], D)).then_inc(ld["gffn"], 16)
            sp.wait_ge(zeros_set, 1)
            sp.dma_start(y_dram[S:S + P, :], zeros[:]).then_inc(st_zero, 16)
            for t in range(T - 1):
                sp.wait_ge(h2_ok, t + 1)
                sp.dma_start(h2_dram[t * P:(t + 1) * P, :], h2[:, t]).then_inc(st_h2, 16)
            sp.wait_ge(out_mm, 2 * T)
            for dst, name in ((ws_g, "w_sh_gate"), (ws_u, "w_sh_up")):
                sp.dma_start(dst[:], a[name][0].rearrange("(p c) n -> p c n", c=C)).then_inc(ld["wsh"], 16)
            sp.wait_ge(h2_ok, T)
            sp.dma_start(h2_dram[(T - 1) * P:T * P, :], h2[:, T - 1]).then_inc(st_h2, 16)
            sp.dma_start(ws_d[:], a["w_sh_down"][0].rearrange("(p c) n -> p c n", c=FC)).then_inc(ld["wsd"], 16)

            def load_gate_up(e, i, half):
                for m, w in enumerate(("w_exp_gate", "w_exp_up")):
                    src = a[w][0, bass.ds(e, 1)].rearrange("o (p c) n -> p (o c) n", c=C)[:, half * HC:(half + 1) * HC, :]
                    sp.dma_start(w_gu[half][i][:, m], src).then_inc(ld_gu[half][i], 16)

            def load_down(e, i):
                sp.dma_start(w_d[i][:], a["w_exp_down"][0, bass.ds(e, 1)].rearrange("o (p c) n -> p (o c) n", c=FC)).then_inc(ld_d[i], 16)

            def down_step(E):
                wait(sp, d_low_ok, num(E, -1))
                apart(sp, "sp")
                load_down(num(E), E[1] % 2)

            def step(E):
                for half in range(2):
                    wait(sp, gu_low_ok[half], num(E, -1))
                    apart(sp, "sp")
                    load_gate_up(num(E), E[1] % 2, half)
                if not (E[0] is None and E[1] == 0):
                    down_step(after(E, -1))

            every_expert(sp, step)
            down_step((None, NE - 1))

            def extra(i):
                e = sp.value_load(list_i[0:1, bass.ds(i, 1)], min_val=0, max_val=NE - 1)
                sp.wait_ge(d_mm, i + NE)
                apart(sp, "sp")
                load_gate_up(e, 0, 0)
                load_gate_up(e, 0, 1)
                load_down(e, 0)

            n = extra_blocks(sp, extra)
            sp.wait_ge(st_y, n * 16 + 16 * NE)
            apart(sp, "sp")
            for t in range(T):
                rows = slice(t * P, (t + 1) * P)
                sp.dma_start(out.rearrange("b s d -> (b s) d")[rows, :], y_dram[rows, :]).then_inc(st_out, 16)
            sp.wait_ge(st_out, 16 * T)

        @block.gpsimd
        def _(pool):
            pool.memset(ones[:], 1.0).then_inc(consts, 1)
            pool.memset(epsc[:], EPS).then_inc(consts, 1)
            pool.wait_ge(consts, 2)
            pool.affine_select(out=ident[:], in_=ones[:], compare_op=ALU.is_equal, fill=0.0, base=0, pattern=[[-1, P]], channel_multiplier=1).then_inc(consts, 1)
            pool.iota(tok[:], pattern=[[P, T]], base=0, channel_multiplier=1, allow_small_or_imprecise_dtypes=True).then_inc(consts, 1)
            for i in range(RH):
                last = pool.memset(freq[:, i:i + 1], float(inv_freq[i]))
            last.then_inc(consts, 1)
            pool.affine_select(out=tri[:], in_=ones[:], compare_op=ALU.is_gt, fill=0.0, base=0, pattern=[[1, P]], channel_multiplier=-1).then_inc(consts, 1)
            pool.affine_select(out=gtri[:], in_=ones[:, 0:N_GROUPS ** 2].rearrange("p (a b) -> p a b", a=N_GROUPS), compare_op=ALU.is_gt, fill=0.0, base=0,
                               pattern=[[1, N_GROUPS], [-1, N_GROUPS]], channel_multiplier=0).then_inc(consts, 1)
            pool.iota(iota[:], pattern=[[1, P]], base=0, channel_multiplier=0, allow_small_or_imprecise_dtypes=True).then_inc(consts, 1)
            pool.iota(part[:], pattern=[[0, 1]], base=0, channel_multiplier=1, allow_small_or_imprecise_dtypes=True).then_inc(consts, 1)
            pool.iota(spare[:], pattern=[[0, 1]], base=S, channel_multiplier=1, allow_small_or_imprecise_dtypes=True).then_inc(consts, 1)
            pool.wait_ge(ld["ws"], 16)
            pool.affine_select(out=ws_low[:], in_=ws_raw[:], compare_op=ALU.is_ge, fill=0.0, base=0, pattern=[[0, GG], [-1, GB]], channel_multiplier=1).then_inc(consts, 1)
            pool.wait_ge(g1_ok, 1)
            pool.memset(bias0[0][:], 0.0)
            pool.memset(bias0[1][:], 0.0).then_inc(bias_zero, 1)
            pool.wait_ge(ld["wq"], 32)
            pool.wait_ge(proj_mm, V0)
            ups = [(w_q_high[:], w_q_low[:], w_q[:])] + [(w_kv_high[c][:], w_kv_low[:, c], w_kv[:, c]) for c in range(KC)]
            for i, (high, low, whole) in enumerate(ups):
                pool.tensor_copy(high, whole).then_inc(wup_high_ok, 1)
                pool.wait_ge(wup_high_ok, i + 1)
                pool.tensor_tensor(low, whole, high.bitcast(F32), ALU.subtract).then_inc(wup_ok, 1)
            for t in range(T):
                pool.wait_ge(proj_ok, (t + 1) * NL)
                if t == 0:
                    pool.wait_ge(ada_dve, len(ADA_DVE))
                pool.tensor_copy(k[:, t, :, NOPE:QD], lat[:, t, QL + KL:LAT].unsqueeze(1).to_broadcast([P, H, ROPE])).then_inc(kpe_ok, 1)

            pool.wait_ge(mod_ok, ADA)
            pool.memset(zeros[:], 0.0).then_inc(zeros_set, 1)
            pool.wait_ge(up_mm, 4 * T)
            for n, i in enumerate((2, 3, 0, 1)):
                if n % 2 == 0:
                    pool.wait_ge(ld_wout[i // 2], 16)
                if n == 2:
                    pool.wait_ge(qkT_tr, 4 * T)
                part_of = slice(i * (C // 4), (i + 1) * (C // 4))
                pool.tensor_copy(w_out_high[i][:], w_out[:, part_of]).then_inc(wout_high_ok, 1)
                pool.wait_ge(wout_high_ok, n + 1)
                pool.tensor_tensor(w_out_low[:, part_of], w_out[:, part_of], w_out_high[i][:].bitcast(F32), ALU.subtract).then_inc(wout_ok, 1)
            pool.wait_ge(selm_ok, 1)
            pool.iota(eblk[:, 0], pattern=[[0, 3], [1, NE]], base=0, channel_multiplier=0, allow_small_or_imprecise_dtypes=True)
            pool.iota(eblk[:, 1], pattern=[[P, 3], [0, NE]], base=P, channel_multiplier=0, allow_small_or_imprecise_dtypes=True).then_inc(pool_step, 1)
            pool.wait_ge(st_h2, 16 * T)

            last_row = pool.to_reg(S - 1)
            last_result = pool.to_reg(S + P - 1)

            def gather(j, i):
                apart(pool, "pool")
                pool.indirect_dma_start(xe[i][:], None, h2_dram, bass.IndirectOffsetOnAxis(ap=src_i[j][:], axis=0),
                                        bounds_check=last_row, oob_is_err=False).then_inc(ld_xe[i], 16)

            def scatter(i):
                apart(pool, "pool")
                pool.indirect_dma_start(y_dram, bass.IndirectOffsetOnAxis(ap=dst_i[i][:], axis=0), oute[i][:], None,
                                        bounds_check=last_result, oob_is_err=False, compute_op=ALU.add).then_inc(st_y, 16)

            pool.wait_ge(h2T_tr, 2 * T)
            pool.wait_ge(st_zero, 16)
            for r in range(3):
                pool.wait_ge(idx_ok, r + 1)
                if r == 2:
                    pool.wait_ge(xeT_tr, 1)
                gather(r % 4, r % 2)

            def step(E):
                G = after(E, 3)
                if exists(G):
                    pool.wait_ge(idx_ok, num(G, 1))
                    pool.wait_ge(xeT_tr, num(G, -1))
                    gather(G[1] % 4, G[1] % 2)
                if first(E):
                    for t in range(T):
                        pool.wait_ge(sh_ok, t + 1)
                        pool.dma_start(y_dram[t * P:(t + 1) * P, :], x[:, t]).then_inc(st_x, 16)
                    pool.wait_ge(st_x, 16 * T)
                pool.wait_ge(oute_ok, num(E, 1))
                wait(pool, st_y, times(num(E), 16))
                scatter(E[1] % 2)

            every_expert(pool, step)

            def extra(i):
                pool.wait_ge(idx_ok, i + (NE + 1))
                gather(0, 0)
                pool.wait_ge(oute_ok, i + (NE + 1))
                pool.wait_ge(st_y, i * 16 + 16 * NE)
                scatter(0)

            extra_blocks(pool, extra)

        @block.tensor
        def _(pe):
            def three_passes(dst, xh, xl, wh, wl, start, stop):
                pe.matmul(dst, xh, wh, start=start, stop=False)
                pe.matmul(dst, xh, wl, start=False, stop=False)
                return pe.matmul(dst, xl, wh, start=False, stop=stop)

            def bias_row(j):
                pe.matmul(bank[j % 2][:], ident[0:ADA, j:j + 1].to_broadcast([ADA, P]), b_ada[0:ADA, :], start=False, stop=True).then_inc(ada_mm, 1)

            pe.wait_ge(consts, 3)
            pe.wait_ge(cbc_ok, 1)
            pe.wait_ge(ld["bada"], 16)
            def ada_sum(j):
                n = ADA_DVE.index(j)
                pe.wait_ge(acc_ok, n + 1)
                if j >= 2:
                    pe.wait_ge(mod_ok, j - 1)
                if j < ADA_FIRST:
                    pe.matmul(bank[j % 2][:], ones[:], acc[n % 2][:], start=True, stop=False)
                    bias_row(j)
                else:
                    pe.matmul(bank[j % 2][:], ones[:], acc[n % 2][:], start=True, stop=True).then_inc(ada_mm, 1)

            for j in range(ADA_FIRST):
                if j == 2:
                    pe.wait_ge(consts, 11)
                    for g in range(GG):
                        last = pe.transpose(bank[2][:, g * GB:(g + 1) * GB], ws_low[:, g, :], ident[:])
                    last.then_inc(wsT_tr, 1)
                if j in ADA_DVE:
                    ada_sum(j)
                    continue
                buf, loads = ada_buffer(j)
                pe.wait_ge(ld_ada[buf], loads)
                if j >= 2:
                    pe.wait_ge(mod_ok, j - 1)
                for c in range(C):
                    last = pe.matmul(bank[j % 2][:], cbc[:, c, :], ada_w[buf][:, c, :], start=(c == 0), stop=False)
                last.then_inc(ada_pe, 1)
                bias_row(j)
            def h_transposes(t):
                pe.wait_ge(h_ok, t + 1)
                for half in range(2):
                    i = 2 * t + half
                    if i >= 2:
                        pe.wait_ge(hT_ok, i - 1)
                    for c4 in range(4):
                        last = pe.transpose(bank[6 + half][:, c4 * P:(c4 + 1) * P], h[:, t, half * 4 + c4::C], ident[:])
                    last.then_inc(hT_tr, 1)

            def projection(i, t, w, n0, n1):
                if i >= 4:
                    pe.wait_ge(proj_ok, i - 3)
                for c in range(C):
                    last = pe.matmul(bank[2 + i % 4][:, 0:n1 - n0], hT[:, c, t * P:(t + 1) * P], w[:, c, n0:n1], start=(c == 0), stop=(c == C - 1))
                last.then_inc(proj_mm, 1)

            h_transposes(0)
            h_transposes(1)
            pe.wait_ge(ld["wlat"], 16)
            pe.wait_ge(wsT_ok, 1)
            for t in range(T):
                pe.wait_ge(hT_ok, 2 * t + 2)
                for m, (n0, n1) in enumerate(lat_cuts):
                    projection(t * NL + m, t, w_lat, n0, n1)
                if t + 2 < T:
                    h_transposes(t + 2)
                ada_sum(ADA_FIRST + t)
            pe.wait_ge(ld["wv"], 16)
            for t in range(T):
                projection(V0 + t, t, w_v, 0, GW)
                ada_sum(ADA_FIRST + T + t)
            pe.wait_ge(latn_ok, 1)
            pe.wait_ge(proj_ok, V0 + T)
            for c in range(QC + KC):
                for t in range(T):
                    src = lat[:, t, c:QL:QC] if c < QC else lat[:, t, QL + c - QC:QL + KL:KC]
                    last = pe.transpose(bank[2 + c][:, t * P:(t + 1) * P], src, ident[:])
                last.then_inc(latT_tr, 1)
            pe.wait_ge(wup_ok, 1 + KC)
            pe.wait_ge(latT_low_ok, QC + KC)
            pe.wait_ge(mod_ok, ADA)
            HQ, HK = H // 2 * QD, H // 2 * KVD
            for t in range(T):
                for m in range(4):
                    i = 4 * t + m
                    if i >= 8:
                        pe.wait_ge(up_ok, i - 7)
                    c0, cn, n0, n1 = (0, QC, m * HQ, (m + 1) * HQ) if m < 2 else (QC, KC, (m - 2) * HK, (m - 1) * HK)
                    tokens = slice(t * P, (t + 1) * P)
                    for c in range(cn):
                        wh, wl = (w_q_high[:, c, n0:n1], w_q_low[:, c, n0:n1]) if m < 2 else (w_kv_high[c][:, n0:n1], w_kv_low[:, c, n0:n1])
                        last = three_passes(bank[i % 8][:, 0:n1 - n0], latT_high[:, c0 + c, tokens], latT_low[c0 + c][:, tokens], wh, wl, c == 0, c == cn - 1)
                    last.then_inc(up_mm, 1)
            pe.wait_ge(ld["wu"], 16)
            pe.wait_ge(up_ok, 4 * T)
            for t in range(T):
                projection(U0 + t, t, w_u, 0, GW)

            def head_transposes(s, src):
                pe.wait_ge(qk_ok, s + 1)
                for t in range(T):
                    for half in range(2):
                        i = s * 2 * T + 2 * t + half
                        if i >= 4:
                            pe.wait_ge(qkT_ok, i - 3)
                        for hh in range(4):
                            last = pe.transpose(bank[2 + i % 4][0:QD, hh * P:(hh + 1) * P], src[:, t, half * 4 + hh, :], ident[:])
                        last.then_inc(qkT_tr, 1)

            pe.wait_ge(proj_ok, U0 + T)
            head_transposes(0, q)
            pe.wait_ge(v_ok, 1)
            for g in range(GG):
                pe.matmul(bank[(7, 0, 1, 6)[g]][:], ws_raw[:, g, :], v[:, :, g * P:(g + 1) * P], start=True, stop=True).then_inc(gate_mm, 1)
            head_transposes(1, k)
            pe.wait_ge(qkT_ok, 4 * T)
            pe.wait_ge(gate_ok, GG)

            def scores(i):
                t, hd = divmod(i, H)
                if i >= NSB:
                    pe.wait_ge(exp_ok, i - NSB + 1)
                pe.matmul(bank[i % NSB][:, 0:(t + 1) * P], qT[0:QD, hd, t * P:(t + 1) * P], kT[0:QD, hd, 0:(t + 1) * P], start=True, stop=True).then_inc(s_mm, 1)

            def prob_transposes(i):
                t, hd = divmod(i, H)
                pe.wait_ge(exp_ok, i + 1)
                if i >= NTB:
                    pe.wait_ge(pT_ok, i - NTB + 1)
                for kb in range(t + 1):
                    last = pe.transpose(bank[NSB + i % NTB][:, kb * P:(kb + 1) * P], prob[i % NPB][:, kb * P:(kb + 1) * P], ident[:])
                last.then_inc(pT_tr, 1)

            def weighted_values(i):
                t, hd = divmod(i, H)
                pe.wait_ge(pT_ok, i + 1)
                if hd == 0 and t >= 2:
                    pe.wait_ge(o_ok, t - 1)
                for kb in range(t + 1):
                    last = pe.matmul(bank[6 + t % 2][:, hd * VD:(hd + 1) * VD], probT[i % NPB][:, kb * P:(kb + 1) * P], vv[:, kb, hd, :], start=(kb == 0), stop=(kb == t))
                last.then_inc(av_mm, 1)

            for i in range(NSB - 1):
                scores(i)
            prob_transposes(0)
            for i in range(NI):
                if i + NSB - 1 < NI:
                    scores(i + NSB - 1)
                if i + 1 < NI:
                    prob_transposes(i + 1)
                weighted_values(i)
            pe.wait_ge(mix_ok, 1)
            pe.wait_ge(mix_v, 1)
            for c in range(C):
                if c >= 6:
                    pe.wait_ge(mixT_low_ok, c - 5)
                for t in range(T):
                    last = pe.transpose(bank[c % 6][:, t * P:(t + 1) * P], mixed[:, t, c::C], ident[:])
                last.then_inc(mixT_tr, 1)
            pe.wait_ge(wout_ok, 4)
            pe.wait_ge(mixT_low_ok, C)
            for t in range(T):
                tokens = slice(t * P, (t + 1) * P)
                for m in range(2):
                    i = 2 * t + m
                    cols = slice(m * BANK, (m + 1) * BANK)
                    if i >= 4:
                        pe.wait_ge(x1_ok, i - 3)
                    for c in range(C):
                        last = three_passes(bank[i % 4][:], mixT_high[:, c, tokens], mixT_low[:, c, tokens],
                                            w_out_high[c // 2][:, c % 2, cols], w_out_low[:, c, cols], c == 0, c == C - 1)
                    last.then_inc(out_mm, 1)
            def h2_transposes(t):
                pe.wait_ge(h2_ok, t + 1)
                for half in range(2):
                    i = 2 * t + half
                    if i >= 2:
                        pe.wait_ge(h2T_ok, i - 1)
                    for c4 in range(4):
                        last = pe.transpose(bank[4 + i % 2][:, c4 * P:(c4 + 1) * P], h2[:, t, half * 4 + c4::C], ident[:])
                    last.then_inc(h2T_tr, 1)

            pe.wait_ge(ld["wr"], 16)
            h2_transposes(0)
            for t in range(T):
                if t + 1 < T:
                    h2_transposes(t + 1)
                pe.wait_ge(h2T_ok, 2 * t + 2)
                for c in range(C):
                    last = pe.matmul(bank[6][:, t * NE:(t + 1) * NE], h2T[:, c, t * P:(t + 1) * P], w_r[:, c, :], start=(c == 0), stop=(c == C - 1))
            last.then_inc(rt_mm, 1)

            def shared_gu(t):
                if t >= 2:
                    pe.wait_ge(shw_ok, t - 1)
                for m, w in enumerate((ws_g, ws_u)):
                    for c in range(C):
                        last = pe.matmul(bank[4 + t % 2][:, m * FF:(m + 1) * FF], h2T[:, c, t * P:(t + 1) * P], w[:, c, :], start=(c == 0), stop=(c == C - 1))
                last.then_inc(sgu_mm, 1)

            def shared_hT(t):
                pe.wait_ge(shw_ok, t + 1)
                for j in range(FC):
                    last = pe.transpose(bank[7][:, j * P:(j + 1) * P], hw[t % 2][:, j::FC], ident[:])
                last.then_inc(shT_tr, 1)

            def shared_down(t):
                if t == 1:
                    pe.wait_ge(xe_low_ok, 4)
                pe.wait_ge(shT_ok, t + 1)
                if t in (1, 2):
                    pe.wait_ge(sh_ok, t)
                for m in range(2):
                    for j in range(FC):
                        last = pe.matmul(bank[shared_banks(t)[m]][:], hwT[:, j, :], ws_d[:, j, m * BANK:(m + 1) * BANK], start=(j == 0), stop=(j == FC - 1))
                last.then_inc(sd_mm, 1)

            pe.wait_ge(ld["wsh"], 32)
            pe.wait_ge(x1_ok, 2 * T)
            shared_gu(0)
            shared_gu(1)
            pe.wait_ge(selm_ok, 1)
            pe.wait_ge(sco_ok, 1)
            for t in range(T):
                for t2 in range(t + 1):
                    pe.matmul(bank[6][:, t * NE:(t + 1) * NE], tri[:] if t2 == t else ones[:], selm[:, t2, :], start=(t2 == 0), stop=(t2 == t))
            for t in range(T):
                last = pe.matmul(bank[6][:, T * NE:(T + 1) * NE], ones[:], selm[:, t, :], start=(t == 0), stop=(t == T - 1))
            last.then_inc(pos_mm, 1)

            def indices(i, e, n):
                pe.wait_ge(oh_ok, n + 1)
                wait(pe, idx_ok, n)
                for t in range(T):
                    last = pe.matmul(bank[6][:, 0:2], onehot[i][:, t, :], pay[:, t, bass.ds(e, 1), :].rearrange("p o c -> p (o c)"), start=(t == 0), stop=(t == T - 1))
                last.then_inc(idx_mm, 1)

            def rows_T(i, loads, n):
                pe.wait_ge(ld_xe[i], loads)
                wait(pe, xe_high_ok, times(n, 2))
                wait(pe, xe_low_ok, times(n, 2))
                for c in range(C):
                    last = pe.transpose(bank[c // 4][:, c % 4 * P:(c % 4 + 1) * P], xe[i][:, c::C], ident[:])
                last.then_inc(xeT_tr, 1)

            def gate_up(i, n, before):
                pe.wait_ge(xe_low_ok, times(n, 2) + 2)
                wait(pe, hw_ok, before)
                for half in range(2):
                    pe.wait_ge(gu_low_ok[half], n + 1)
                    for c in range(HC):
                        last = three_passes(bank[2 + i][:], xeT_high[i][:, half * HC + c, :], xeT_low[i][:, half * HC + c, :],
                                            gu_high[half][:, :, c, :], gu_low[half][:, :, c, :], half == 0 and c == 0, half == 1 and c == HC - 1)
                    last.then_inc((gu_mm0, gu_mm)[half], 1)

            def hidden_T(i, n):
                pe.wait_ge(hw_ok, n + 1)
                wait(pe, hwT_low_ok, n)
                for j in range(FC):
                    last = pe.transpose(bank[7][:, j * P:(j + 1) * P], hw[i][:, j::FC], ident[:])
                last.then_inc(hwT_tr, 1)

            def down(n):
                pe.wait_ge(d_low_ok, n + 1)
                pe.wait_ge(hwT_low_ok, n + 1)
                wait(pe, oute_ok, n)
                for m in range(2):
                    cols = slice(m * BANK, (m + 1) * BANK)
                    for j in range(FC):
                        last = three_passes(bank[4 + m][:], hwT_high[:, j, :], hwT_low[:, j, :], d_high[:, j, cols], d_low[:, j, cols], j == 0, j == FC - 1)
                last.then_inc(d_mm, 1)

            def rows_T_of(E):
                rows_T(E[1] % 2, times(pairs(E), 16), num(E))

            def gate_up_of(E):
                gate_up(E[1] % 2, num(E), num(E, -1))

            shared_hT(0)
            pe.wait_ge(ld["wsd"], 16)
            shared_down(0)
            pe.wait_ge(pay_ok, 1)
            for r in range(3):
                indices(r % 2, r, r)
            pe.wait_ge(lmat_ok, 1)
            pe.wait_ge(idx_ok, 3)
            pe.matmul(bank[6][:, 0:2 * MAXX], ones[0:MAXX, :], lmat[0:MAXX], start=True, stop=True).then_inc(list_mm, 1)
            rows_T_of((None, 0))
            shared_gu(2)
            rows_T_of((None, 1))
            pe.wait_ge(sh_ok, 1)
            gate_up_of((None, 0))
            shared_hT(1)
            shared_down(1)
            shared_gu(3)
            pe.wait_ge(list_ok, 2)
            indices(1, 3, 3)
            gate_up_of((None, 1))
            for t in range(2, T):
                shared_hT(t)
                shared_down(t)
            pe.wait_ge(sh_ok, T)

            def step(E):
                if exists(after(E, 3)) and not first(E):
                    indices((E[1] + 3) % 2, num(E, 3), num(E, 3))
                hidden_T(E[1] % 2, num(E))
                if exists(after(E, 1)) and not first(E):
                    gate_up_of(after(E, 1))
                if exists(after(E, 2)):
                    rows_T_of(after(E, 2))
                down(num(E))

            every_expert(pe, step)

            def extra(i):
                e = pe.value_load(list_i[0:1, bass.ds(i, 1)], min_val=0, max_val=NE - 1)
                n = i + NE
                indices(0, e, n)
                rows_T(0, i * 16 + 16 * (EXTRA0 + 1), n)
                gate_up(0, n, n)
                hidden_T(0, n)
                down(n)

            extra_blocks(pe, extra)

        @block.scalar
        def _(act):
            act.dma_start(b_ada[0:ADA, :], a["b_ada"].rearrange("l (j n) -> (l j) n", n=BANK)).then_inc(ld["bada"], 16)
            act.dma_start(posi[:], a["positions"].rearrange("b (t p) -> p (b t)", p=P), allow_slow_non_contiguous=True).then_inc(ld["pos"], 16)
            act.dma_start(gmix[:], bcast(a["norm_mix_g"], D)).then_inc(ld["gmix"], 16)
            act.dma_start(ws_raw[:], a["gm_ws"].rearrange("l g t s -> t (l g) s")).then_inc(ld["ws"], 16)
            smalls = [
                (ln_g[:], bcast(a["gm_ln_g"].rearrange("l g c -> l (g c)"), GW)),
                (ln_b[:], bcast(a["gm_ln_b"].rearrange("l g c -> l (g c)"), GW)),
                (bsT[:], a["gm_bs"].rearrange("l g t -> t (l g)")),
                (qa_g[:], a["q_a_g"].rearrange("l (p c) -> p (l c)", c=QC)),
                (kva_g[:], a["kv_a_g"].rearrange("l (p c) -> p (l c)", c=KC)),
                (qn_g[:], bcast(a["q_norm_g"], QD)),
                (kn_g[:], bcast(a["k_norm_g"], QD)),
                (on_g[:], a["out_norm_g"].rearrange("l (p c) -> p (l c)", c=C)),
                (rbias[:], bcast(a["router_bias"], NE)),
            ]
            assert len(smalls) == NSMALL
            for dst, src in smalls:
                act.dma_start(dst, src, allow_slow_non_contiguous=True).then_inc(ld["small"], 16)
            act.wait_ge(ld["c"], 16)
            act.activation(cact[:], cT[:], ACT.Silu).then_inc(silu_c, 1)
            act.wait_ge(ang_ok, 1)
            act.activation(sin[:], ang[:], ACT.Sin).then_inc(trig_ok, 1)
            act.activation(cos[:], turns[:], ACT.Sin).then_inc(trig_ok, 1)

            def copy_mod(j):
                act.wait_ge(ada_mm, j + 1)
                act.copy(mod[:, j // 2, j % 2 * BANK:(j % 2 + 1) * BANK], bank[j % 2][:]).then_inc(mod_ok, 1)

            act.wait_ge(ss_ok, 1)
            act.wait_ge(consts, 2)
            act.activation(ss[:], ss[:], ACT.Sqrt, bias=epsc[:], scale=1.0 / D).then_inc(std_ok, 1)
            for j in range(ADA_FIRST):
                copy_mod(j)
            def hT_copy(t):
                for half in range(2):
                    act.wait_ge(hT_tr, 2 * t + half + 1)
                    act.copy(hT[:, half * 4:half * 4 + 4, t * P:(t + 1) * P], bank[6 + half][:].rearrange("p (c n) -> p c n", c=4)).then_inc(hT_ok, 1)

            hT_copy(0)
            hT_copy(1)
            for t in range(T):
                for m, (n0, n1) in enumerate(lat_cuts):
                    i = t * NL + m
                    act.wait_ge(proj_mm, i + 1)
                    act.copy(lat[:, t, n0:n1], bank[2 + i % 4][:, 0:n1 - n0]).then_inc(proj_ok, 1)
                if t + 2 < T:
                    hT_copy(t + 2)
                copy_mod(ADA_FIRST + t)
            act.wait_ge(stats_ok, 1)
            act.activation(latss[:, :, 0], latss[:, :, 0], ACT.Sqrt, bias=epsc[:], scale=1.0 / QL).then_inc(lstd_ok, 1)
            act.activation(latss[:, :, 1], latss[:, :, 1], ACT.Sqrt, bias=epsc[:], scale=1.0 / KL).then_inc(lstd_ok, 1)
            act.wait_ge(lrstd_ok, 1)
            for t in range(T):
                for s, (n0, n1) in enumerate(((0, QL), (QL, QL + KL))):
                    last = act.activation(lat[:, t, n0:n1], lat[:, t, n0:n1], ACT.Copy, scale=latss[:, t, s:s + 1])
            last.then_inc(latn_ok, 1)

            def gelu(dst, i, t):
                act.wait_ge(proj_mm, i + 1)
                act.activation(dst[:, t, :], bank[2 + i % 4][:, 0:GW], ACT.Gelu).then_inc(proj_ok, 1)

            for t in range(T):
                gelu(v, V0 + t, t)
                copy_mod(ADA_FIRST + T + t)
            for c in range(QC + KC):
                act.wait_ge(latT_tr, c + 1)
                gain = qa_g[:, c:c + 1] if c < QC else kva_g[:, c - QC:c - QC + 1]
                if c == 0:
                    act.wait_ge(ld["small"], 16 * NSMALL)
                    act.wait_ge(ada_dve, len(ADA_DVE))
                act.activation(latT_high[:, c, :], bank[2 + c][:], ACT.Copy, scale=gain).then_inc(latT_ok, 1)
            act.wait_ge(vstats_ok, 1)
            act.activation(lnmv[:, :, 1], lnmv[:, :, 1], ACT.Sqrt, bias=epsc[:]).then_inc(vstd_ok, 1)
            act.wait_ge(kpe_ok, T)
            HH = H // 2
            for t in range(T):
                for m in range(4):
                    i = 4 * t + m
                    act.wait_ge(up_mm, i + 1)
                    if m < 2:
                        act.copy(q[:, t, m * HH:(m + 1) * HH, :], bank[i % 8][:, 0:HH * QD].rearrange("p (h d) -> p h d", h=HH)).then_inc(up_ok, 1)
                    else:
                        src = bank[i % 8][:].rearrange("p (h d) -> p h d", h=HH)
                        act.copy(k[:, t, (m - 2) * HH:(m - 1) * HH, 0:NOPE], src[:, :, 0:NOPE])
                        act.copy(vv[:, t, (m - 2) * HH:(m - 1) * HH, :], src[:, :, NOPE:KVD]).then_inc(up_ok, 1)
                for s, z in enumerate((q, k)):
                    if t:
                        act.wait_ge(ssq_ok, 2 * (t - 1) + s + 1)
                    act.wait_ge(up_ok, 4 * t + 2 * s + 2)
                    act.activation(sq[:, s], z[:, t], ACT.Square).then_inc(sq_ok, 1)
            act.wait_ge(ssq_ok, 2 * T)
            act.activation(qkss[:], qkss[:], ACT.Sqrt, bias=epsc[:], scale=1.0 / QD).then_inc(qstd_ok, 1)
            act.wait_ge(g1_ok, 1)
            for t in range(T):
                gelu(u, U0 + t, t)
            for i in range(4 * T):
                s, r = divmod(i, 2 * T)
                t, half = divmod(r, 2)
                act.wait_ge(qkT_tr, i + 1)
                if s and r == 0:
                    act.wait_ge(gate_ok, GG)
                act.copy((qT, kT)[s][0:QD, half * 4:half * 4 + 4, t * P:(t + 1) * P], bank[2 + i % 4][0:QD, :].rearrange("p (h n) -> p h n", h=4)).then_inc(qkT_ok, 1)
            def exponential(i):
                t, hd = divmod(i, H)
                act.wait_ge(nmax_ok, i + 1)
                if i >= NPB:
                    act.wait_ge(pT_tr, i - NPB + 1)
                act.activation(prob[i % NPB][:, 0:(t + 1) * P], bank[i % NSB][:, 0:(t + 1) * P], ACT.Exp, bias=nmax[:, t, hd:hd + 1],
                               accum_out=den[:, t, hd:hd + 1]).then_inc(exp_ok, 1)

            def prob_copy(i):
                t, hd = divmod(i, H)
                act.wait_ge(pT_tr, i + 1)
                if i >= NPB:
                    act.wait_ge(av_mm, i - NPB + 1)
                act.copy(probT[i % NPB][:, 0:(t + 1) * P], bank[NSB + i % NTB][:, 0:(t + 1) * P]).then_inc(pT_ok, 1)

            exponential(0)
            for i in range(NI):
                if i + 1 < NI:
                    exponential(i + 1)
                prob_copy(i)
            act.wait_ge(oss_ok, 1)
            act.activation(oss[:], oss[:], ACT.Sqrt, bias=epsc[:], scale=1.0 / GW).then_inc(ostd_ok, 1)
            act.wait_ge(orstd_ok, 1)
            for t in range(T):
                last = act.activation(mixed[:, t, GW:D], mixed[:, t, GW:D], ACT.Copy, scale=oss[:, t, 1:2])
            last.then_inc(mix_ok, 1)
            for c in range(C):
                act.wait_ge(mixT_tr, c + 1)
                act.activation(mixT_high[:, c, :], bank[c % 6][:], ACT.Copy, scale=on_g[:, c:c + 1]).then_inc(mixT_high_ok, 1)
            def std2(t):
                act.wait_ge(ss2_ok, t + 1)
                act.activation(ss[:, t:t + 1], ss[:, t:t + 1], ACT.Sqrt, bias=epsc[:], scale=1.0 / D).then_inc(std2_ok, 1)

            for t in range(T - 1):
                std2(t)
            for t in range(T):
                if t == 1:
                    std2(T - 1)
                for half in range(2):
                    i = 2 * t + half
                    act.wait_ge(h2T_tr, i + 1)
                    act.copy(h2T[:, half * 4:half * 4 + 4, t * P:(t + 1) * P], bank[4 + i % 2][:].rearrange("p (c n) -> p c n", c=4)).then_inc(h2T_ok, 1)
            act.wait_ge(rt_mm, 1)
            act.wait_ge(st_h2, 16 * T)
            act.activation(sco[:], bank[6][:, 0:T * NE].rearrange("p (t e) -> p t e", t=T), ACT.Sigmoid).then_inc(sco_ok, 1)
            def shared_silu(t):
                act.wait_ge(sgu_mm, t + 1)
                if t >= 2:
                    act.wait_ge(shw_ok, t - 1)
                act.activation(sgate[t % 2][:], bank[4 + t % 2][:, 0:FF], ACT.Silu).then_inc(ssilu_ok, 1)

            def shared_hT_copy(t):
                act.wait_ge(shT_tr, t + 1)
                if t:
                    act.wait_ge(sd_mm, t)
                act.copy(hwT[:], bank[7][:, 0:FC * P].rearrange("p (j n) -> p j n", j=FC)).then_inc(shT_ok, 1)

            def gate_up_high(half, i, loads, n):
                act.wait_ge(ld_gu[half][i], loads)
                wait(act, (gu_mm0, gu_mm)[half], n)
                for m in range(2):
                    act.copy(gu_high[half][:, m], w_gu[half][i][:, m]).then_inc(gu_high_ok[half], 1)

            def down_high(i, loads, n):
                act.wait_ge(ld_d[i], loads)
                wait(act, d_mm, n)
                for m in range(2):
                    act.copy(d_high[:, m], w_d[i][:, m]).then_inc(d_high_ok, 1)

            def rows_high(i, n):
                act.wait_ge(xeT_tr, n + 1)
                for m in range(2):
                    act.copy(xeT_high[i][:, m * HC:(m + 1) * HC, :], bank[m][:].rearrange("p (c n) -> p c n", c=HC)).then_inc(xe_high_ok, 1)

            def silu(i, n, free):
                act.wait_ge(gu_mm, n + 1)
                wait(act, hw_ok, free)
                act.activation(sgate[i][:], bank[2 + i][:, 0:FF], ACT.Silu).then_inc(silu_ok, 1)

            def hidden_high(n):
                act.wait_ge(hwT_tr, n + 1)
                wait(act, d_mm, n)
                act.copy(hwT_high[:], bank[7][:, 0:FC * P].rearrange("p (j n) -> p j n", j=FC)).then_inc(hwT_high_ok, 1)

            def gate_up_high_of(half, E):
                gate_up_high(half, E[1] % 2, times(pairs(E), 32), num(E))

            def down_high_of(E):
                down_high(E[1] % 2, times(pairs(E), 16), num(E))

            def rows_high_of(E):
                if not (E[0] is None and E[1] < 2):
                    act.wait_ge(gu_mm, num(E, -1))
                rows_high(E[1] % 2, num(E))

            act.wait_ge(h2_ok, T)
            gate_up_high_of(0, (None, 0))
            gate_up_high_of(1, (None, 0))
            shared_silu(0)
            shared_silu(1)
            shared_hT_copy(0)
            act.wait_ge(list_ok, 2)
            act.wait_ge(pay_ok, 1)
            rows_high_of((None, 0))
            shared_silu(2)
            rows_high_of((None, 1))
            shared_hT_copy(1)
            gate_up_high_of(0, (None, 1))
            gate_up_high_of(1, (None, 1))
            shared_silu(3)
            down_high_of((None, 0))
            gate_up_high_of(0, (None, 2))
            shared_hT_copy(2)
            act.wait_ge(shw_ok, 3)
            silu(0, 0, 0)
            gate_up_high_of(1, (None, 2))
            shared_hT_copy(3)
            act.wait_ge(shw_ok, T)

            def step(E):
                E1, E2 = after(E, 1), after(E, 2)
                hidden_high(num(E))
                if exists(E2) and not first(E):
                    gate_up_high_of(0, E2)
                if exists(E1):
                    silu(E1[1] % 2, num(E1), num(E1, -1))
                if exists(E2):
                    rows_high_of(E2)
                if exists(E2) and not first(E):
                    gate_up_high_of(1, E2)
                if exists(E1):
                    down_high_of(E1)

            every_expert(act, step)

            def extra(i):
                n = i + NE
                gate_up_high(0, 0, i * 32 + 32 * (EXTRA0 + 1), n)
                gate_up_high(1, 0, i * 32 + 32 * (EXTRA0 + 1), n)
                down_high(0, i * 16 + 16 * (EXTRA0 + 1), n)
                rows_high(0, n)
                silu(0, n, n)
                hidden_high(n)

            extra_blocks(act, extra)

        @block.vector
        def _(dve):
            steps = [0]

            def link(ins):
                steps[0] += 1
                ins.then_inc(dve_step, 1)
                dve.wait_ge(dve_step, steps[0])

            dve.wait_ge(silu_c, 1)
            dve.tensor_copy(cbc[:], cact[:].unsqueeze(2).to_broadcast([P, C, P])).then_inc(cbc_ok, 1)
            dve.wait_ge(ld["pos"], 16)
            dve.wait_ge(consts, 5)
            link(dve.tensor_copy(posf[:], posi[:]))
            link(dve.tensor_tensor(ang[:], posf[:].unsqueeze(2).to_broadcast([P, T, RH]), freq[:].unsqueeze(1).to_broadcast([P, T, RH]), ALU.mult))
            link(dve.tensor_scalar(turns[:], ang[:], float(1.0 / (2 * np.pi)), MAGIC, ALU.mult, ALU.add))
            link(dve.tensor_scalar(turns[:], turns[:], -MAGIC, None, ALU.add))
            for piece in TWO_PI:
                link(dve.scalar_tensor_tensor(ang[:], turns[:], -piece, ang[:], ALU.mult, ALU.add))
            link(dve.tensor_scalar(ang[:], ang[:], PI_BELOW, -PI_BELOW, ALU.min, ALU.max))
            link(dve.scalar_tensor_tensor(turns[:], ang[:], -1.0, ang[:], ALU.mult, ALU.max))
            dve.tensor_scalar(turns[:], turns[:], -1.0, float(np.pi / 2), ALU.mult, ALU.add).then_inc(ang_ok, 1)
            def ada_block(j):
                n = ADA_DVE.index(j)
                buf, loads = ada_buffer(j)
                dve.wait_ge(ld_ada[buf], loads)
                if n >= 2:
                    dve.wait_ge(ada_mm, ADA_DVE[n - 2] + 1)
                w = ada_w[buf]
                if j < ADA_FIRST:
                    link(dve.tensor_scalar(acc[n % 2][:], w[:, 0, :], cact[:, 0:1], None, ALU.mult))
                else:
                    dve.wait_ge(ld_bias[j % 2], 16 * ((j - ADA_FIRST) // 2 + 1))
                    link(dve.scalar_tensor_tensor(acc[n % 2][:], w[:, 0, :], cact[:, 0:1], bias0[j % 2][:], ALU.mult, ALU.add))
                for c in range(1, C):
                    ins = dve.scalar_tensor_tensor(acc[n % 2][:], w[:, c, :], cact[:, c:c + 1], acc[n % 2][:], ALU.mult, ALU.add)
                    if c < C - 1:
                        link(ins)
                ins.then_inc(acc_ok, 1)
                dve.wait_ge(acc_ok, n + 1)
                dve.engine_nop().then_inc(ada_dve, 1)

            ada_block(1)
            dve.wait_ge(ld["x"], 16)
            for t in range(T):
                last = dve.tensor_tensor_reduce(h[:, t], x[:, t], x[:, t], 1.0, 0.0, ALU.mult, ALU.add, ss[:, t:t + 1])
            last.then_inc(ss_ok, 1)
            dve.wait_ge(std_ok, 1)
            link(dve.reciprocal(ss[:], ss[:]))
            dve.wait_ge(wsT_tr, 1)
            dve.tensor_copy(ws_raw[:], bank[2][:].rearrange("p (g n) -> p g n", g=GG)).then_inc(wsT_ok, 1)
            ada_block(3)
            dve.wait_ge(mod_ok, ADA_FIRST)
            dve.wait_ge(ld["gmix"], 16)
            dve.scalar_tensor_tensor(mod[:, G1], mod[:, G1], 1.0, gmix[:], ALU.add, ALU.mult).then_inc(g1_ok, 1)
            dve.wait_ge(g1_ok, 1)
            for t in range(T):
                link(dve.scalar_tensor_tensor(h[:, t], x[:, t], ss[:, t:t + 1], mod[:, G1], ALU.mult, ALU.mult))
                dve.tensor_tensor(h[:, t], h[:, t], mod[:, SH1], ALU.add).then_inc(h_ok, 1)

            for t in range(T):
                ada_block(ADA_FIRST + t)
                dve.wait_ge(proj_ok, NL * (t + 1))
                link(dve.tensor_tensor_reduce(lsq[:, 0:QL], lat[:, t, 0:QL], lat[:, t, 0:QL], 1.0, 0.0, ALU.mult, ALU.add, latss[:, t, 0:1]))
                last = dve.tensor_tensor_reduce(lsq[:, 0:KL], lat[:, t, QL:QL + KL], lat[:, t, QL:QL + KL], 1.0, 0.0, ALU.mult, ALU.add, latss[:, t, 1:2])
                if t < T - 1:
                    link(last)
            last.then_inc(stats_ok, 1)
            dve.wait_ge(lstd_ok, 2)
            dve.reciprocal(latss[:], latss[:]).then_inc(lrstd_ok, 1)
            for t in range(T):
                ada_block(ADA_FIRST + T + t)
            for c in range(QC + KC):
                dve.wait_ge(latT_ok, c + 1)
                gain = qa_g[:, c:c + 1] if c < QC else kva_g[:, c - QC:c - QC + 1]
                dve.scalar_tensor_tensor(latT_low[c][:], bank[2 + c][:], gain, latT_high[:, c, :].bitcast(F32), ALU.mult, ALU.subtract).then_inc(latT_low_ok, 1)
            for t in range(T):
                dve.wait_ge(proj_ok, V0 + t + 1)
                for g in range(GG):
                    last = dve.bn_stats(lnst[:, t * GG + g, :], v[:, t, g * P:(g + 1) * P])
            link(last)
            for i in range(T * GG):
                last = dve.bn_aggr(lnmv[:, i, :], lnst[:, i, :])
            last.then_inc(vstats_ok, 1)
            dve.wait_ge(vstd_ok, 1)
            link(dve.reciprocal(lnmv[:, :, 1], lnmv[:, :, 1]))
            dve.wait_ge(ld["small"], 16 * NSMALL)
            for t in range(T):
                for g in range(GG):
                    s = t * GG + g
                    last = dve.tensor_scalar(v[:, t, g * P:(g + 1) * P], v[:, t, g * P:(g + 1) * P], lnmv[:, s, 0:1], lnmv[:, s, 1:2], ALU.subtract, ALU.mult)
            link(last)
            link(dve.tensor_tensor(v[:], v[:], ln_g[:].unsqueeze(1).to_broadcast([P, T, GW]), ALU.mult))
            dve.tensor_tensor(v[:], v[:], ln_b[:].unsqueeze(1).to_broadcast([P, T, GW]), ALU.add).then_inc(v_ok, 1)
            link(dve.tensor_scalar(qn_g[:], qn_g[:], scale, None, ALU.mult))
            for i in range(2 * T):
                t, s = divmod(i, 2)
                dve.wait_ge(sq_ok, i + 1)
                dve.tensor_reduce(qkss[:, s, t, :], sq[:, s], AX.X, ALU.add).then_inc(ssq_ok, 1)
            dve.wait_ge(qstd_ok, 1)
            link(dve.reciprocal(qkss[:], qkss[:]))
            dve.wait_ge(trig_ok, 2)
            dve.wait_ge(ssq_ok, 2 * T)
            for s, (z, gain) in enumerate(((q, qn_g), (k, kn_g))):
                for t in range(T):
                    last = dve.tensor_tensor(z[:, t], z[:, t], qkss[:, s, t, :].unsqueeze(2).to_broadcast([P, H, QD]), ALU.mult)
                link(last)
                for t in range(T):
                    last = dve.tensor_tensor(z[:, t], z[:, t], gain[:].unsqueeze(1).to_broadcast([P, H, QD]), ALU.mult)
                link(last)
                z1, z2 = z[:, :, :, NOPE:NOPE + RH], z[:, :, :, NOPE + RH:QD]
                cb = cos[:].unsqueeze(2).to_broadcast([P, T, H, RH])
                sb_ = sin[:].unsqueeze(2).to_broadcast([P, T, H, RH])
                dve.tensor_tensor(rt[0][:], z1, cb, ALU.mult)
                dve.tensor_tensor(rt[1][:], z2, sb_, ALU.mult)
                dve.tensor_tensor(rt[2][:], z1, sb_, ALU.mult)
                link(dve.tensor_tensor(rt[3][:], z2, cb, ALU.mult))
                dve.tensor_tensor(z1, rt[0][:], rt[1][:], ALU.subtract)
                dve.tensor_tensor(z2, rt[2][:], rt[3][:], ALU.add).then_inc(qk_ok, 1)
                dve.wait_ge(qk_ok, s + 1)

            dve.wait_ge(proj_ok, U0 + T)
            for g in range(GG):
                dve.wait_ge(gate_mm, g + 1)
                dve.scalar_tensor_tensor(mixed[:, :, g * P:(g + 1) * P], bank[(7, 0, 1, 6)[g]][:].rearrange("p (t n) -> p t n", t=T), bsT[:, g:g + 1],
                                         u[:, :, g * P:(g + 1) * P], ALU.add, ALU.mult).then_inc(gate_ok, 1)

            def row_max(i):
                t, hd = divmod(i, H)
                dve.wait_ge(s_mm, i + 1)
                link(dve.memset(bank[i % NSB][0:CHUNK, t * P + CHUNK:(t + 1) * P], NEG))
                dve.tensor_reduce(nmax[:, t, hd:hd + 1], bank[i % NSB][:, 0:(t + 1) * P], AX.X, ALU.max, negate=True).then_inc(nmax_ok, 1)

            def outputs(t):
                dve.wait_ge(av_mm, (t + 1) * H)
                link(dve.reciprocal(den[:, t, :], den[:, t, :]))
                dve.tensor_tensor(mixed[:, t, GW:D].rearrange("p (h d) -> p h d", h=H), bank[6 + t % 2][:].rearrange("p (h d) -> p h d", h=H),
                                  den[:, t, :].unsqueeze(2).to_broadcast([P, H, VD]), ALU.mult).then_inc(o_ok, 1)
                dve.wait_ge(o_ok, t + 1)
                for s in range(2):
                    last = dve.tensor_tensor_reduce(osq[:, s * GW:(s + 1) * GW], mixed[:, t, s * GW:(s + 1) * GW], mixed[:, t, s * GW:(s + 1) * GW], 1.0, 0.0, ALU.mult, ALU.add, oss[:, t, s:s + 1])
                if t < T - 1:
                    link(last)
                else:
                    last.then_inc(oss_ok, 1)

            dve.wait_ge(gate_ok, GG)
            for i in range(NI):
                row_max(i)
                if i % H == 3 and i > H:
                    outputs(i // H - 1)
            outputs(T - 1)
            dve.wait_ge(ostd_ok, 1)
            dve.reciprocal(oss[:], oss[:]).then_inc(orstd_ok, 1)
            dve.wait_ge(orstd_ok, 1)
            for t in range(T):
                last = dve.tensor_scalar(mixed[:, t, 0:GW], mixed[:, t, 0:GW], oss[:, t, 0:1], None, ALU.mult)
            last.then_inc(mix_v, 1)
            for c in range(C):
                dve.wait_ge(mixT_high_ok, c + 1)
                dve.scalar_tensor_tensor(mixT_low[:, c, :], bank[c % 6][:], on_g[:, c:c + 1], mixT_high[:, c, :].bitcast(F32), ALU.mult, ALU.subtract).then_inc(mixT_low_ok, 1)
            dve.wait_ge(ld["gffn"], 16)
            dve.wait_ge(mod_ok, ADA)
            dve.scalar_tensor_tensor(mod[:, G2], mod[:, G2], 1.0, gffn[:], ALU.add, ALU.mult).then_inc(g2_ok, 1)
            dve.wait_ge(g2_ok, 1)

            def residual(t):
                for m in range(2):
                    i = 2 * t + m
                    cols = slice(m * BANK, (m + 1) * BANK)
                    dve.wait_ge(out_mm, i + 1)
                    dve.tensor_tensor(xtmp[:, cols], bank[i % 4][:], mod[:, GATE1, cols], ALU.mult).then_inc(x1_ok, 1)
                    dve.wait_ge(x1_ok, i + 1)
                    link(dve.tensor_tensor(x[:, t, cols], x[:, t, cols], xtmp[:, cols], ALU.add))
                dve.tensor_tensor_reduce(h2[:, t], x[:, t], x[:, t], 1.0, 0.0, ALU.mult, ALU.add, ss[:, t:t + 1]).then_inc(ss2_ok, 1)

            def norm2(t):
                dve.wait_ge(std2_ok, t + 1)
                link(dve.reciprocal(ss[:, t:t + 1], ss[:, t:t + 1]))
                link(dve.scalar_tensor_tensor(h2[:, t], x[:, t], ss[:, t:t + 1], mod[:, G2], ALU.mult, ALU.mult))
                dve.tensor_tensor(h2[:, t], h2[:, t], mod[:, SH2], ALU.add).then_inc(h2_ok, 1)

            for t in range(T):
                residual(t)
                norm2(t)
            dve.wait_ge(sco_ok, 1)
            dve.wait_ge(st_h2, 16 * T)
            dve.wait_ge(h2T_tr, 2 * T)
            link(dve.tensor_tensor(bia[:], sco[:], rbias[:].unsqueeze(1).to_broadcast([P, T, NE]), ALU.add))
            for i in range(T * N_GROUPS):
                t, g = divmod(i, N_GROUPS)
                last = dve.max(m8[:, i, :], bia[:, t, g * EG:(g + 1) * EG])
            link(last)
            link(dve.tensor_tensor(gsum[:].rearrange("p t g -> p (t g)"), m8[:, :, 0], m8[:, :, 1], ALU.add))
            other = gsum[:].unsqueeze(2).to_broadcast([P, T, N_GROUPS, N_GROUPS])
            own = gsum[:].unsqueeze(3).to_broadcast([P, T, N_GROUPS, N_GROUPS])
            dve.tensor_tensor(cgt[:], other, own, ALU.is_gt)
            link(dve.tensor_tensor(cge[:], other, own, ALU.is_ge))
            link(dve.tensor_tensor(cge[:], cge[:], gtri[:].unsqueeze(1).to_broadcast([P, T, N_GROUPS, N_GROUPS]), ALU.mult))
            link(dve.tensor_tensor(cge[:], cge[:], cgt[:], ALU.max))
            link(dve.tensor_reduce(grank[:], cge[:], AX.X, ALU.add))
            link(dve.tensor_scalar(gmask[:], grank[:], float(TOPK_GROUPS) - 0.5, None, ALU.is_lt))
            link(dve.tensor_scalar(gneg[:], gmask[:], 1.0, -NEG, ALU.subtract, ALU.mult))
            ge = lambda z: z[:].rearrange("p t (g e) -> p t g e", g=N_GROUPS)
            eb = lambda z: z[:].unsqueeze(3).to_broadcast([P, T, N_GROUPS, EG])
            link(dve.tensor_tensor(ge(bia), ge(bia), eb(gmask), ALU.mult))
            link(dve.tensor_tensor(ge(bia), ge(bia), eb(gneg), ALU.add))
            for t in range(T):
                last = dve.max(v8[:, t, :], bia[:, t, :])
            link(last)
            for t in range(T):
                last = dve.match_replace(rep[:, t, :], v8[:, t, :], bia[:, t, :], 4.0 * NEG)
            link(last)
            dve.tensor_tensor(selm[:], rep[:], bia[:], ALU.not_equal).then_inc(selm_ok, 1)
            dve.wait_ge(selm_ok, 1)
            link(dve.tensor_tensor(comb[:], selm[:], sco[:], ALU.mult))
            link(dve.tensor_reduce(wsum[:], comb[:], AX.X, ALU.add))
            link(dve.reciprocal(wsum[:], wsum[:]))
            link(dve.scalar_tensor_tensor(pay[:, :, :, 1], comb[:], ROUTED_SCALE, wsum[:].unsqueeze(2).to_broadcast([P, T, NE]), ALU.mult, ALU.mult))
            link(dve.memset(zero[:], 0.0))
            link(dve.tensor_scalar(pay[:, :, :, 0], tok[:].unsqueeze(2).to_broadcast([P, T, NE]), -BIG, None, ALU.add))

            def shared_hidden(t):
                dve.wait_ge(ssilu_ok, t + 1)
                if t >= 2:
                    dve.wait_ge(shT_tr, t - 1)
                dve.tensor_tensor(hw[t % 2][:], bank[4 + t % 2][:, FF:2 * FF], sgate[t % 2][:], ALU.mult).then_inc(shw_ok, 1)

            def shared_out(t):
                dve.wait_ge(sd_mm, t + 1)
                for m in range(2):
                    last = dve.tensor_tensor(xtmp[:, m * BANK:(m + 1) * BANK], bank[shared_banks(t)[m]][:], mod[:, GATE2, m * BANK:(m + 1) * BANK], ALU.mult)
                link(last)
                dve.tensor_tensor(x[:, t], x[:, t], xtmp[:], ALU.add).then_inc(sh_ok, 1)
                dve.wait_ge(sh_ok, t + 1)

            iota_b = iota[:].unsqueeze(1).to_broadcast([P, T, P])

            def one_hot(i, slots, n):
                wait(dve, idx_mm, n + (-1))
                dve.tensor_tensor(onehot[i][:], slots.to_broadcast([P, T, P]), iota_b, ALU.is_equal).then_inc(oh_ok, 1)

            def index_rows(j, n):
                dve.wait_ge(idx_mm, n + 1)
                dve.tensor_scalar(src_i[j][:], bank[6][:, 0:1], BIG, None, ALU.add)
                dve.tensor_copy(slots[j][:], bank[6][:, 0:2]).then_inc(idx_ok, 1)

            def lowered(low, whole, high):
                return dve.tensor_tensor(low, whole, high.bitcast(F32), ALU.subtract)

            def gate_up_low(half, i, n):
                wait(dve, (gu_mm0, gu_mm)[half], n)
                for m in range(2):
                    dve.wait_ge(gu_high_ok[half], times(n, 2) + (m + 1))
                    last = lowered(gu_low[half][:, m], w_gu[half][i][:, m], gu_high[half][:, m])
                last.then_inc(gu_low_ok[half], 1)

            def down_low(i, n):
                wait(dve, d_mm, n)
                for m in range(2):
                    dve.wait_ge(d_high_ok, times(n, 2) + (m + 1))
                    last = lowered(d_low[:, m], w_d[i][:, m], d_high[:, m])
                last.then_inc(d_low_ok, 1)

            def rows_low(i, n):
                for m in range(2):
                    dve.wait_ge(xe_high_ok, times(n, 2) + (m + 1))
                    lowered(xeT_low[i][:, m * HC:(m + 1) * HC, :], bank[m][:].rearrange("p (c n) -> p c n", c=HC), xeT_high[i][:, m * HC:(m + 1) * HC, :]).then_inc(xe_low_ok, 1)

            def hidden(j, i, n):
                dve.wait_ge(silu_ok, n + 1)
                dve.wait_ge(idx_ok, n + 1)
                wait(dve, hwT_tr, n + (-1))
                dve.scalar_tensor_tensor(hw[i][:], bank[2 + i][:, FF:2 * FF], slots[j][:, 1:2], sgate[i][:], ALU.mult, ALU.mult).then_inc(hw_ok, 1)

            def hidden_low(n):
                wait(dve, d_mm, n)
                dve.wait_ge(hwT_high_ok, n + 1)
                lowered(hwT_low[:], bank[7][:, 0:FC * P].rearrange("p (j n) -> p j n", j=FC), hwT_high[:]).then_inc(hwT_low_ok, 1)

            def out_copy(j, i, n, stores):
                dve.wait_ge(d_mm, n + 1)
                wait(dve, st_y, stores)
                dve.tensor_scalar(dst_i[i][:], slots[j][:, 0:1], BIG, spare[:], ALU.add, ALU.min)
                for m in range(2):
                    cols = slice(m * BANK, (m + 1) * BANK)
                    last = dve.tensor_tensor(oute[i][:, cols], bank[4 + m][:], mod[:, GATE2, cols], ALU.mult)
                last.then_inc(oute_ok, 1)

            def one_hot_of(E):
                one_hot(E[1] % 2, posm[:, :, bass.ds(num(E), 1)], num(E))

            def gate_up_low_of(half, E):
                gate_up_low(half, E[1] % 2, num(E))

            def rows_low_of(E):
                if not (E[0] is None and E[1] < 2):
                    dve.wait_ge(gu_mm, num(E, -1))
                rows_low(E[1] % 2, num(E))

            shared_hidden(0)
            gate_up_low_of(0, (None, 0))
            gate_up_low_of(1, (None, 0))
            dve.wait_ge(pos_mm, 1)
            pos = bank[6][:, 0:T * NE].rearrange("p (t e) -> p t e", t=T)
            dve.tensor_copy(cnt[:], bank[6][:, T * NE:(T + 1) * NE])
            link(dve.scalar_tensor_tensor(posm[:], pos, 1.0, selm[:], ALU.add, ALU.mult))
            dve.tensor_scalar(posm[:], posm[:], -1.0, None, ALU.add).then_inc(pay_ok, 1)
            dve.wait_ge(pay_ok, 1)

            one_hot_of((None, 0))
            one_hot_of((None, 1))
            index_rows(0, 0)
            one_hot_of((None, 2))
            index_rows(1, 1)
            dve.wait_ge(pool_step, 1)
            for b in range(3):
                last = dve.tensor_scalar(flag[:, b * NE:(b + 1) * NE], cnt[:], float((b + 1) * P) + 0.5, None, ALU.is_gt)
            link(last)
            link(dve.tensor_tensor_scan(runs[:], flag[:], zero[:], 0.0, ALU.add, ALU.add))
            dve.tensor_copy(nextra[:], runs[:, 3 * NE - 1:3 * NE]).then_inc(list_ok, 1)
            dve.wait_ge(list_ok, 1)
            link(dve.tensor_scalar(runs[:], runs[:], part[:], 1.0, ALU.subtract, ALU.is_equal))
            link(dve.tensor_tensor(flag[:], flag[:], runs[:], ALU.mult))
            for s in range(2):
                link(dve.tensor_tensor_reduce(ltmp[:], flag[:], eblk[:, s].rearrange("p b e -> p (b e)"), 1.0, 0.0, ALU.mult, ALU.add, lcol[:, s:s + 1]))
            for s in range(2):
                last = dve.tensor_scalar(lmat[0:MAXX, s, :], ident[0:MAXX, 0:MAXX], lcol[0:MAXX, s:s + 1], None, ALU.mult)
            last.then_inc(lmat_ok, 1)
            index_rows(2, 2)
            one_hot_of((None, 3))
            dve.wait_ge(list_mm, 1)
            dve.tensor_copy(list_i[:], bank[6][:, 0:2 * MAXX])
            dve.tensor_copy(list_f[:], bank[6][:, 0:2 * MAXX]).then_inc(list_ok, 1)
            rows_low_of((None, 0))
            shared_hidden(1)
            shared_out(0)
            shared_hidden(2)
            rows_low_of((None, 1))
            gate_up_low_of(0, (None, 1))
            gate_up_low_of(1, (None, 1))
            shared_out(1)
            shared_hidden(3)
            index_rows(3, 3)
            one_hot_of((None, 4))
            down_low(0, 0)
            gate_up_low_of(0, (None, 2))
            dve.wait_ge(shT_tr, 3)
            hidden(0, 0, 0)
            gate_up_low_of(1, (None, 2))
            shared_out(2)
            shared_out(3)

            def step(E):
                E1, E2, E3, E4 = (after(E, d) for d in (1, 2, 3, 4))
                if exists(E3) and not first(E):
                    wait(dve, oute_ok, num(E))
                    index_rows(E3[1] % 4, num(E3))
                hidden_low(num(E))
                if exists(E4) and not first(E):
                    one_hot_of(E4)
                if exists(E2) and not first(E):
                    gate_up_low_of(0, E2)
                if exists(E1):
                    hidden(E1[1] % 4, E1[1] % 2, num(E1))
                if exists(E2):
                    rows_low_of(E2)
                if exists(E2) and not first(E):
                    gate_up_low_of(1, E2)
                out_copy(E[1] % 4, E[1] % 2, num(E), times(num(E, -1), 16))
                if exists(E1):
                    down_low(E1[1] % 2, num(E1))

            every_expert(dve, step)

            def extra(i):
                e = dve.value_load(list_i[0:1, bass.ds(i, 1)], min_val=0, max_val=NE - 1)
                n = i + NE
                dve.wait_ge(st_y, i * 16 + 16 * NE)
                dve.wait_ge(idx_mm, n)
                dve.tensor_scalar(posx[:], posm[:, :, bass.ds(e, 1)].rearrange("p t o -> p (t o)"), list_f[:, bass.ds(i + MAXX, 1)], None, ALU.subtract).then_inc(posx_ok, 1)
                dve.wait_ge(posx_ok, i + 1)
                one_hot(0, posx[:].unsqueeze(2), n)
                index_rows(0, n)
                gate_up_low(0, 0, n)
                gate_up_low(1, 0, n)
                down_low(0, n)
                rows_low(0, n)
                hidden(0, 0, n)
                hidden_low(n)
                out_copy(0, 0, n, i * 16 + 16 * NE)

            extra_blocks(dve, extra)


def times(n, by):
    return n * by


def kernel(**inputs):
    import concourse.bacc as bacc
    from concourse.bass_utils import run_bass_kernel_spmd

    nc = bacc.Bacc("TRN2", target_bir_lowering=False, num_devices=1)
    arrays = {f"in_{name}": np.ascontiguousarray(v) for name, v in inputs.items()}
    aps = {name: nc.dram_tensor(f"in_{name}", inputs[name].shape, mybir.dt.from_np(arrays[f"in_{name}"].dtype), kind="ExternalInput").ap() for name in inputs}
    out = nc.dram_tensor("out", inputs["x"].shape, F32, kind="ExternalOutput").ap()
    trunk_kernel(nc, aps, out)
    r = run_bass_kernel_spmd(nc, [arrays], core_ids=[0])
    return r.results[0]["out"]
```
